# Optimizing a Trainium2 kernel written in Bass

```python
import jax
import jax.numpy as jnp
from jax import lax
import numpy as np

D_MODEL = 1024
BATCH = 1
SEQ = 128
DEPTH = 2
DEC_BATCH = 1
DEC_SEQ = 256
PAST_LEN = 128

GRID_W = 64
N_BRANCH = 3
D_A = D_MODEL // 2
N_A = 64
H_A = D_A // N_A
W_LORA = 64
A_LORA = 64
G_LORA = 128
D_B = D_MODEL // 2
DH_B = 64
H_B = D_B // DH_B
NA_KH = 8
NA_KW = 16
D_C = D_MODEL // 2
DH_C = 64
H_C = D_C // DH_C
RET_CHUNK = 64
D_FF = 2816
ROPE_BASE = 10000.0
QBLOCK = 128
RWKV_COLS = 3 * D_A + W_LORA + A_LORA + G_LORA
NA_COLS = 3 * D_B
RET_COLS = 4 * D_C
GATE_COLS = N_BRANCH * D_MODEL
IN_COLS = RWKV_COLS + NA_COLS + RET_COLS + GATE_COLS
NEG_BIG = -1e9
RWKV_LN_EPS = 64e-5
RET_GN_EPS = 1e-5
F32 = jnp.float32

kernel_name = 'hybrid_rwkv7_natten_retention_diffusion_step'

def rmsnorm(x, g, eps=1e-6):
    xf = x.astype(F32)
    y = xf * lax.rsqrt(jnp.mean(xf * xf, axis=-1, keepdims=True) + eps)
    return (y * g.astype(F32)).astype(x.dtype)

def head_groupnorm(y, eps):
    B, T, H, Dh = y.shape
    yf = y.astype(F32)
    mu = jnp.mean(yf, axis=-1, keepdims=True)
    var = jnp.mean(jnp.square(yf - mu), axis=-1, keepdims=True)
    return ((yf - mu) * lax.rsqrt(var + eps)).reshape(B, T, H * Dh)

def dwconv3(x, w):
    xp = jnp.pad(x, ((0, 0), (1, 1), (0, 0)))
    return xp[:, :-2] * w[0] + xp[:, 1:-1] * w[1] + xp[:, 2:] * w[2]

def ada_modulation(cvec, w, b):
    m = jax.nn.silu(cvec) @ w + b
    return m.reshape(m.shape[0], 6, D_MODEL)

def axial_rope(x):
    B, T, H, Dh = x.shape
    t = jnp.arange(T)
    half = Dh // 2
    nf = half // 2
    inv = ROPE_BASE ** (-jnp.arange(nf, dtype=F32) / nf)

    def rot(xp, pos):
        ang = pos.astype(F32)[:, None] * inv[None, :]
        cos = jnp.cos(ang)[None, :, None, :]
        sin = jnp.sin(ang)[None, :, None, :]
        x1 = xp[..., :nf].astype(F32)
        x2 = xp[..., nf:].astype(F32)
        return jnp.concatenate([x1 * cos - x2 * sin, x1 * sin + x2 * cos], axis=-1)

    out = jnp.concatenate([rot(x[..., :half], t // GRID_W), rot(x[..., half:], t % GRID_W)], axis=-1)
    return out.astype(x.dtype)

def wkv7_scan(r, w, k, v, a, b, s0, reverse):
    xs = tuple(jnp.moveaxis(t.astype(F32), 1, 0) for t in (r, w, k, v, a, b))

    def step(S, inp):
        r_t, w_t, k_t, v_t, a_t, b_t = inp
        sa = jnp.einsum('bhvk,bhk->bhv', S, a_t)
        S = S * w_t[:, :, None, :] + sa[..., None] * b_t[:, :, None, :] + v_t[..., None] * k_t[:, :, None, :]
        return S, jnp.einsum('bhvk,bhk->bhv', S, r_t)

    S, ys = lax.scan(step, s0.astype(F32), xs, reverse=reverse)
    return jnp.moveaxis(ys, 0, 1), S

def rwkv7_branch(z, s0, lp):
    B, T, _ = z.shape
    r, k, v, wl, al, gl = jnp.split(z, [D_A, 2 * D_A, 3 * D_A, 3 * D_A + W_LORA, 3 * D_A + W_LORA + A_LORA], axis=-1)
    heads = lambda t: t.reshape(B, T, H_A, N_A)
    kk = heads(k * lp['rwkv_k_k']).astype(F32)
    kk = kk / jnp.maximum(jnp.sqrt(jnp.sum(kk * kk, axis=-1, keepdims=True)), 1e-12)
    g = jax.nn.sigmoid(gl) @ lp['rwkv_g_up']
    wt = jnp.tanh(wl)
    ys = []
    states = []
    for d in range(2):
        w_log = -jax.nn.softplus(-(lp['rwkv_w0'][d] + wt @ lp['rwkv_w_up'][d]).astype(F32)) - 0.5
        decay = jnp.exp(-jnp.exp(w_log))
        a = jax.nn.sigmoid((lp['rwkv_a0'][d] + al @ lp['rwkv_a_up'][d]).astype(F32))
        k_d = k.astype(F32) * (1.0 + (a - 1.0) * lp['rwkv_k_a'].astype(F32))
        y_d, s_d = wkv7_scan(heads(r), heads(decay), heads(k_d), heads(v), -kk, kk * heads(a), s0[:, d], d == 1)
        ys.append(y_d)
        states.append(s_d)
    y = ys[0] + ys[1]
    bonus = jnp.sum(heads(r) * heads(k) * lp['rwkv_r_k'], axis=-1, keepdims=True) * heads(v)
    o = head_groupnorm(y, RWKV_LN_EPS) * lp['rwkv_ln_g'].astype(F32) + lp['rwkv_ln_b'].astype(F32)
    o = (o.astype(z.dtype) + bonus.reshape(B, T, D_A)) * g
    return o @ lp['w_o_rwkv'], jnp.stack(states, axis=1).astype(s0.dtype)

def dense_attention(q, k, v):
    B, L, H, D = q.shape
    qb = q.reshape(B, L // QBLOCK, QBLOCK, H, D).transpose(1, 0, 2, 3, 4)

    def block(qi):
        s = jnp.einsum('bqhd,bhkd->bhqk', qi, k).astype(F32) * (D ** -0.5)
        p = jax.nn.softmax(s, axis=-1).astype(v.dtype)
        return jnp.einsum('bhqk,bhkd->bqhd', p, v)

    o = lax.map(block, qb)
    return o.transpose(1, 0, 2, 3, 4).reshape(B, L, H, D)

def neighbourhood_attention(q, k, v, k_ctx, v_ctx, rpb):
    B, T, H, D = q.shape
    rows = T // GRID_W
    kh = min(NA_KH, rows)
    scale = D ** -0.5
    qg = q.reshape(B, rows, GRID_W, H, D).transpose(1, 0, 2, 3, 4)
    kg = k.reshape(B, rows, GRID_W, H, D)
    vg = v.reshape(B, rows, GRID_W, H, D)
    cols = jnp.arange(GRID_W)
    c_start = jnp.clip(cols - NA_KW // 2, 0, GRID_W - NA_KW)
    col_valid = (cols[None, :] >= c_start[:, None]) & (cols[None, :] < c_start[:, None] + NA_KW)
    dc = jnp.clip(cols[None, :] - cols[:, None], -(NA_KW - 1), NA_KW - 1) + NA_KW - 1
    r_idx = jnp.arange(rows)
    r_start = jnp.clip(r_idx - kh // 2, 0, rows - kh)

    def row_block(args):
        q_r, r, rs = args
        k_r = lax.dynamic_slice_in_dim(kg, rs, kh, axis=1)
        v_r = lax.dynamic_slice_in_dim(vg, rs, kh, axis=1)
        dr = rs + jnp.arange(kh) - r + NA_KH - 1
        bias = rpb[:, dr[None, :, None], dc[:, None, :]].astype(F32)
        s_loc = jnp.einsum('bqhd,bjwhd->bhqjw', q_r, k_r).astype(F32) * scale + bias[None]
        s_loc = jnp.where(col_valid[:, None, :], s_loc, NEG_BIG).reshape(B, H, GRID_W, kh * GRID_W)
        s_ctx = jnp.einsum('bqhd,bhld->bhql', q_r, k_ctx).astype(F32) * scale
        p = jax.nn.softmax(jnp.concatenate([s_loc, s_ctx], axis=-1), axis=-1).astype(v.dtype)
        o = jnp.einsum('bhqn,bnhd->bqhd', p[..., :kh * GRID_W], v_r.reshape(B, kh * GRID_W, H, D))
        return o + jnp.einsum('bhql,bhld->bqhd', p[..., kh * GRID_W:], v_ctx)

    o = lax.map(row_block, (qg, r_idx, r_start))
    return o.transpose(1, 0, 2, 3, 4).reshape(B, T, H, D)

def retention_chunkwise(q, k, v, log_gamma, s0):
    B, T, H, Dh = q.shape
    n = T // RET_CHUNK
    j = jnp.arange(RET_CHUNK, dtype=F32)
    diff = j[:, None] - j[None, :]
    dmat = jnp.where(diff >= 0, jnp.exp(log_gamma[:, None, None] * jnp.maximum(diff, 0.0)), 0.0)
    xi = jnp.exp(log_gamma[:, None] * (j + 1.0))[:, :, None]
    zeta = jnp.exp(log_gamma[:, None] * (RET_CHUNK - 1.0 - j))[:, :, None]
    g_chunk = jnp.exp(log_gamma * RET_CHUNK)[:, None, None]

    def chunks(t):
        return t.astype(F32).reshape(B, n, RET_CHUNK, H, Dh).transpose(1, 0, 3, 2, 4)

    def step(S, inp):
        qi, ki, vi = inp
        inner = jnp.einsum('bhid,bhjd->bhij', qi, ki) * dmat
        o = jnp.einsum('bhij,bhjv->bhiv', inner, vi) + jnp.einsum('bhid,bhdv->bhiv', qi, S) * xi
        S = S * g_chunk + jnp.einsum('bhjd,bhjv->bhdv', ki * zeta, vi)
        return S, o

    S, o = lax.scan(step, s0.astype(F32), (chunks(q), chunks(k), chunks(v)))
    return o.transpose(1, 0, 3, 2, 4).reshape(B, T, H, Dh), S

def retention_branch(z, s0, lp, use_rope):
    B, T, _ = z.shape
    q, k, v, g = jnp.split(z, 4, axis=-1)
    q, k, v = (t.reshape(B, T, H_C, DH_C) for t in (q, k, v))
    if use_rope:
        q, k = axial_rope(q), axial_rope(k)
    k = k * (DH_C ** -0.5)
    lg = jax.nn.log_sigmoid(lp['ret_decay'].astype(F32))
    y_f, s_f = retention_chunkwise(q, k, v, lg[0], s0[:, 0])
    y_b, s_b = retention_chunkwise(jnp.flip(q, 1), jnp.flip(k, 1), jnp.flip(v, 1), lg[1], s0[:, 1])
    y = y_f + jnp.flip(y_b, 1)
    o = (head_groupnorm(y, RET_GN_EPS) * lp['ret_gn'].astype(F32)).astype(z.dtype) * jax.nn.silu(g)
    return o @ lp['w_o_ret'], jnp.stack([s_f, s_b], axis=1).astype(s0.dtype)

def conv_ffn(h, w_up, w_conv, w_down):
    u = dwconv3(h @ w_up, w_conv)
    val, gate = jnp.split(u, 2, axis=-1)
    return (jax.nn.gelu(gate) * val) @ w_down

def trunk_layer(x, m, lp, s_rwkv, s_ret, k_ctx, v_ctx, is_ctx):
    B, T, _ = x.shape
    sh1, sc1, g1, sh2, sc2, g2 = (m[:, i][:, None, :] for i in range(6))
    h = rmsnorm(x, lp['norm_mix_pre']) * (1.0 + sc1) + sh1
    z = h @ lp['w_in']
    o0 = RWKV_COLS
    o1 = o0 + NA_COLS
    o2 = o1 + RET_COLS
    z_rwkv = dwconv3(z[..., :o0], lp['rwkv_conv'])
    z_na = z[..., o0:o1]
    z_ret = z[..., o1:o2]
    gates = jax.nn.sigmoid(z[..., o2:]).reshape(B, T, N_BRANCH, D_MODEL)
    out_a, st_rwkv = rwkv7_branch(z_rwkv, s_rwkv, lp)
    q, k, v = (t.reshape(B, T, H_B, DH_B) for t in jnp.split(z_na, 3, axis=-1))
    if is_ctx:
        k_ctx = k.transpose(0, 2, 1, 3)
        v_ctx = v.transpose(0, 2, 1, 3)
        o_na = dense_attention(q, k_ctx, v_ctx)
    else:
        o_na = neighbourhood_attention(q, k, v, k_ctx, v_ctx, lp['na_rpb'])
    out_b = o_na.reshape(B, T, D_B) @ lp['w_o_na']
    out_c, st_ret = retention_branch(z_ret, s_ret, lp, not is_ctx)
    merged = gates[:, :, 0] * out_a + gates[:, :, 1] * out_b + gates[:, :, 2] * out_c
    x = x + g1 * rmsnorm(merged @ lp['w_out'], lp['norm_mix_post'])
    h2 = rmsnorm(x, lp['norm_ffn_pre']) * (1.0 + sc2) + sh2
    x = x + g2 * rmsnorm(conv_ffn(h2, lp['ffn_up'], lp['ffn_conv'], lp['ffn_down']), lp['norm_ffn_post'])
    return x, st_rwkv, st_ret, k_ctx, v_ctx

def setup_inputs(seed: int = 0) -> dict:
    key = jax.random.key(seed)
    ks = jax.random.split(key, 48)
    cnt = [0]

    def nxt():
        cnt[0] += 1
        return ks[cnt[0] - 1]

    def nrm(shape, scale):
        return jax.random.normal(nxt(), shape, F32) * scale

    def gain(shape):
        return 1.0 + nrm(shape, 0.05)

    def conv3(ch):
        return nrm((DEPTH, 3, ch), 0.2).at[:, 1].add(1.0)

    ret_base = jnp.log(2.0 ** (5.0 + jnp.arange(H_C, dtype=F32)) - 1.0)
    return {
        'x_prompt': nrm((BATCH, SEQ, D_MODEL), 1.0),
        'x_sample': nrm((DEC_BATCH, DEC_SEQ, D_MODEL), 1.0),
        'cache_na_k': nrm((DEC_BATCH, DEPTH, H_B, PAST_LEN, DH_B), 1.0),
        'cache_na_v': nrm((DEC_BATCH, DEPTH, H_B, PAST_LEN, DH_B), 1.0),
        'state_rwkv': nrm((DEC_BATCH, DEPTH, 2, H_A, N_A, N_A), 0.3),
        'state_ret': nrm((DEC_BATCH, DEPTH, 2, H_C, DH_C, DH_C), 0.3),
        'c': nrm((DEC_BATCH, D_MODEL), 1.0),
        'c_ctx': nrm((D_MODEL,), 1.0),
        'ada_w': nrm((DEPTH, D_MODEL, 6 * D_MODEL), D_MODEL ** -0.5),
        'ada_b': nrm((DEPTH, 6 * D_MODEL), 0.01),
        'norm_mix_pre': gain((DEPTH, D_MODEL)),
        'norm_mix_post': gain((DEPTH, D_MODEL)),
        'norm_ffn_pre': gain((DEPTH, D_MODEL)),
        'norm_ffn_post': gain((DEPTH, D_MODEL)),
        'w_in': nrm((DEPTH, D_MODEL, IN_COLS), D_MODEL ** -0.5),
        'rwkv_conv': conv3(RWKV_COLS),
        'rwkv_w0': jax.random.uniform(nxt(), (DEPTH, 2, D_A), F32, -6.0, 1.0),
        'rwkv_w_up': nrm((DEPTH, 2, W_LORA, D_A), 0.5 * W_LORA ** -0.5),
        'rwkv_a0': nrm((DEPTH, 2, D_A), 0.3),
        'rwkv_a_up': nrm((DEPTH, 2, A_LORA, D_A), 0.5 * A_LORA ** -0.5),
        'rwkv_g_up': nrm((DEPTH, G_LORA, D_A), G_LORA ** -0.5),
        'rwkv_k_k': 0.85 + nrm((DEPTH, D_A), 0.05),
        'rwkv_k_a': gain((DEPTH, D_A)),
        'rwkv_r_k': nrm((DEPTH, H_A, N_A), 0.1),
        'rwkv_ln_g': gain((DEPTH, D_A)),
        'rwkv_ln_b': nrm((DEPTH, D_A), 0.01),
        'na_rpb': nrm((DEPTH, H_B, 2 * NA_KH - 1, 2 * NA_KW - 1), 0.1),
        'ret_decay': ret_base + nrm((DEPTH, 2, H_C), 0.05),
        'ret_gn': gain((DEPTH, D_C)),
        'w_o_rwkv': nrm((DEPTH, D_A, D_MODEL), D_A ** -0.5),
        'w_o_na': nrm((DEPTH, D_B, D_MODEL), D_B ** -0.5),
        'w_o_ret': nrm((DEPTH, D_C, D_MODEL), D_C ** -0.5),
        'w_out': nrm((DEPTH, D_MODEL, D_MODEL), D_MODEL ** -0.5),
        'ffn_up': nrm((DEPTH, D_MODEL, 2 * D_FF), D_MODEL ** -0.5),
        'ffn_conv': conv3(2 * D_FF),
        'ffn_down': nrm((DEPTH, D_FF, D_MODEL), D_FF ** -0.5),
    }

def reference(x_prompt, x_sample, cache_na_k, cache_na_v, state_rwkv, state_ret, c,
              c_ctx, ada_w, ada_b, norm_mix_pre, norm_mix_post, norm_ffn_pre, norm_ffn_post,
              w_in, rwkv_conv, rwkv_w0, rwkv_w_up, rwkv_a0, rwkv_a_up, rwkv_g_up,
              rwkv_k_k, rwkv_k_a, rwkv_r_k, rwkv_ln_g, rwkv_ln_b, na_rpb, ret_decay, ret_gn,
              w_o_rwkv, w_o_na, w_o_ret, w_out, ffn_up, ffn_conv, ffn_down):
    bp = x_prompt.shape[0]
    xp = x_prompt
    xs = x_sample
    new_k, new_v, new_rw, new_rt = [], [], [], []
    for l in range(DEPTH):
        lp = {
            'norm_mix_pre': norm_mix_pre[l], 'norm_mix_post': norm_mix_post[l],
            'norm_ffn_pre': norm_ffn_pre[l], 'norm_ffn_post': norm_ffn_post[l],
            'w_in': w_in[l], 'rwkv_conv': rwkv_conv[l], 'rwkv_w0': rwkv_w0[l], 'rwkv_w_up': rwkv_w_up[l],
            'rwkv_a0': rwkv_a0[l], 'rwkv_a_up': rwkv_a_up[l], 'rwkv_g_up': rwkv_g_up[l],
            'rwkv_k_k': rwkv_k_k[l], 'rwkv_k_a': rwkv_k_a[l], 'rwkv_r_k': rwkv_r_k[l],
            'rwkv_ln_g': rwkv_ln_g[l], 'rwkv_ln_b': rwkv_ln_b[l], 'na_rpb': na_rpb[l],
            'ret_decay': ret_decay[l], 'ret_gn': ret_gn[l], 'w_o_rwkv': w_o_rwkv[l], 'w_o_na': w_o_na[l],
            'w_o_ret': w_o_ret[l], 'w_out': w_out[l], 'ffn_up': ffn_up[l], 'ffn_conv': ffn_conv[l],
            'ffn_down': ffn_down[l],
        }
        m_ctx = ada_modulation(c_ctx[None, :], ada_w[l], ada_b[l])
        zero_rw = jnp.zeros((bp, 2, H_A, N_A, N_A), xp.dtype)
        zero_rt = jnp.zeros((bp, 2, H_C, DH_C, DH_C), xp.dtype)
        xp, st_rw, st_rt, k_c, v_c = trunk_layer(xp, m_ctx, lp, zero_rw, zero_rt, None, None, True)
        new_k.append(k_c)
        new_v.append(v_c)
        new_rw.append(st_rw)
        new_rt.append(st_rt)
        m_lat = ada_modulation(c, ada_w[l], ada_b[l])
        xs, _, _, _, _ = trunk_layer(xs, m_lat, lp, state_rwkv[:, l], state_ret[:, l],
                                     cache_na_k[:, l], cache_na_v[:, l], False)
    return (xp, xs, jnp.stack(new_k, axis=1), jnp.stack(new_v, axis=1), jnp.stack(new_rw, axis=1), jnp.stack(new_rt, axis=1))


_drawn_inputs = setup_inputs


def setup_inputs(seed=0):
    import zlib

    import numpy as np

    out = dict(_drawn_inputs(seed))
    spreads = {}
    factors = {'state_rwkv': 8.0, 'rwkv_ln_g': 3.895, 'rwkv_ln_b': 8.0, 'na_rpb': 7.55}
    for name, (base, spread) in spreads.items():
        noise = np.random.default_rng([zlib.crc32(name.encode()), seed]).standard_normal(out[name].shape)
        drawn = base * np.exp(spread * noise) if base else spread * noise
        out[name] = jnp.asarray(drawn.astype(out[name].dtype))
    for name, factor in factors.items():
        out[name] = (out[name] * factor).astype(out[name].dtype)
    return out
```

```python
from contextlib import ExitStack

import concourse.bass as bass
from concourse import mybir

F32 = mybir.dt.float32
U32 = mybir.dt.uint32
ALU = mybir.AluOpType
ACT = mybir.ActivationFunctionType
AX = mybir.AxisListType

P = 128
D = 1024
KT = D // P
DEPTH = 2
SEQ, DEC = 128, 256
GAP = SEQ
LAT = SEQ + 1
TP = SEQ + 1 + DEC
TT = [0, LAT, LAT + P]
CH = 64
PAIRS = 4
FT = 22
DECAY_C = 0.6065306597126334
RING = 6
CN_PAIR = 20
LEVELS = 6
STREAMS = [(0, 1, 0, SEQ), (1, 2, LAT, TP)]

ADA0 = 0
SHARED0 = ADA0 + 48
PAIR0 = SHARED0 + 2
MERGE0 = PAIR0 + 10 * PAIRS
OUT0 = MERGE0 + 36
UP0 = OUT0 + 8
DOWN0 = UP0 + 2 * FT
BLOCKS = DOWN0 + FT

PRM = {}
NPRM = 0
for _name, _n in (("mix_pre", 8), ("mix_post", 8), ("ffn_pre", 8), ("ffn_post", 8), ("ada_b", 48),
                  ("conv", 42), ("fconv", 132), ("w0", 8), ("a0", 8), ("k_k", 4), ("k_a", 4),
                  ("r_k", 4), ("ln_g", 4), ("ln_b", 4), ("gn", 4), ("dec_ch", 8), ("dec_hd", 16)):
    PRM[_name] = NPRM
    NPRM += _n

PK = {}
NPK = 0
for _name, _n in (("lora", 256), ("g_up", 128), ("kc", 128), ("vc", 128), ("bias", 768),
                  ("s_rw", 128), ("s_rt", 128)):
    PK[_name] = NPK
    NPK += _n

CN = {}
NCN = 0
for _name, _n in (("ident", 128), ("ones", 128), ("blk", 128), ("perm", 128), ("cos", 256), ("sin", 256),
                  ("reset", 2 * TP), ("tri", 4 * 128), ("lev", LEVELS * 2 * 128), ("posd", 384),
                  ("negd", 384), ("diag", 384), ("xi", 512), ("colmask", 64), ("zp", 2)):
    CN[_name] = NCN
    NCN += _n


class Signal:

    def __init__(self, handle):
        self.h = handle
        self.n = 0

    def by(self, ins, k=1):
        ins.then_inc(self.h, k)
        self.n += k
        return self.n


class Lane:

    def __init__(self, eng, step, z_free):
        self.eng, self.step, self.z_free = eng, step, z_free

    def do(self, ins, sig=None, free=None):
        if free is not None:
            ins.then_inc(self.z_free[free % 2], 1)
            self.last = self.z_free[free % 2], free // 2 + 1
        else:
            sig = sig or self.step
            self.last = sig.h, sig.by(ins)

    def settle(self):
        self.eng.wait_ge(*self.last)


def trunk(nc, xin, wstream, prm_d, pk_d, cc_d, const_d, x_out, nak, nav, srw, srt):
    ctx = ExitStack()
    with ctx:
        def sb(name, cols, dt=F32):
            return ctx.enter_context(nc.sbuf_tensor(name, [P, cols], dt))

        const = sb("const", NCN)
        xres = sb("xres", KT * TP)
        hbuf = sb("hbuf", KT * TP)
        mix = sb("mix", 3 * PAIRS * TP)
        ring = sb("ring", RING * 1024)
        prm = sb("prm", NPRM)
        pk = sb("pk", NPK)
        cc = sb("cc", 2 * KT)
        small = sb("small", 400)
        WORK = 26902
        work = sb("work", WORK)
        psz = ctx.enter_context(nc.psum_tensor("psz", [P, 2, 512], F32))
        psw = ctx.enter_context(nc.psum_tensor("psw", [P, 6, 512], F32))

        def cv(name, n, a=0):
            return const[:, CN[name] + a:CN[name] + a + n]

        ident, ones, blk, perm = (cv(n, 128) for n in ("ident", "ones", "blk", "perm"))
        cosT, sinT = cv("cos", 256), cv("sin", 256)
        x = [xres[:, k * TP:(k + 1) * TP] for k in range(KT)]
        h = [hbuf[:, k * TP:(k + 1) * TP] for k in range(KT)]
        mixed = [[mix[:, (b * PAIRS + p) * TP:(b * PAIRS + p + 1) * TP] for p in range(PAIRS)] for b in range(3)]
        slot = [ring[:, s * 1024:(s + 1) * 1024].rearrange("p (k c) -> p k c", k=8) for s in range(RING)]

        def par(name, i):
            return prm[:, PRM[name] + i:PRM[name] + i + 1]

        taken = [0]

        def sm(n):
            taken[0] += n
            assert taken[0] <= 400
            return small[:, taken[0] - n:taken[0]]

        mod = sm(96).rearrange("p (m s) -> p m s", s=2)
        scale1 = sm(16).rearrange("p (m s) -> p m s", s=2)
        scale2 = sm(16).rearrange("p (m s) -> p m s", s=2)
        gate1 = sm(16).rearrange("p (m s) -> p m s", s=2)
        gate2 = sm(16).rearrange("p (m s) -> p m s", s=2)
        lg = sm(24)
        lt = sm(24)
        ls = sm(24)
        lq = sm(24)
        omka = sm(4)
        eps_rms = sm(1)
        eps_rw = sm(1)
        eps_rt = sm(1)
        zeta = sm(4)
        pend = sm(12).rearrange("p (d c) -> p d c", d=2)
        mx = sm(2)
        rs = sm(2)
        ri = sm(2)
        mt = sm(2)
        cs = sm(16).rearrange("p (k s) -> p k s", s=2)

        at = [0]

        def wk(n):
            at[0] += n
            assert at[0] <= WORK, at[0]
            return work[:, at[0] - n:at[0]]

        rc, kc_, vc = (wk(TP) for _ in range(3))
        nq, nk = wk(TP), wk(TP)
        nv = wk(384).rearrange("p (t c) -> p t c", t=3)
        tq, tk = wk(TP), wk(TP)
        tv = wk(384).rearrange("p (t c) -> p t c", t=3)
        tg = wk(TP)
        kk, bonus, gr = wk(TP), wk(TP), wk(TP)
        ar = wk(4 * TP).rearrange("p (d k t) -> p d k t", d=2, k=2)
        bk = wk(4 * TP).rearrange("p (d k t) -> p d k t", d=2, k=2)
        bkt = wk(4 * 384).rearrange("p (d k t c) -> p d k t c", d=2, k=2, t=3)
        vt = wk(384).rearrange("p (t c) -> p t c", t=3)
        au = wk(12 * 512).rearrange("p (u k c) -> p u k c", u=12, k=4)
        ut = wk(6 * 128).rearrange("p (d t c) -> p d t c", d=2, t=3)
        g0 = wk(6 * 128).rearrange("p (d t c) -> p d t c", d=2, t=3)
        gs = wk(2 * 128).rearrange("p (s c) -> p s c", s=2)
        st = wk(12 * 128).rearrange("p (d c v) -> p d c v", d=2, c=6)
        stp = wk(4 * 128).rearrange("p (s d v) -> p s d v", s=2, d=2)
        fin = wk(2 * 64).rearrange("p (d v) -> p d v", d=2)
        lwal, lgl = wk(TP), wk(TP)
        dtab = wk(2 * 384).rearrange("p (h c) -> p h c", h=2)
        s0 = wk(2 * 128).rearrange("p (d v) -> p d v", d=2)
        ktz = wk(256).rearrange("p (d c) -> p d c", d=2)
        srtb = wk(2 * 64).rearrange("p (d v) -> p d v", d=2)
        inv0 = at[0]
        tvv = wk(12 * 128).rearrange("p (u c) -> p u c", u=12)
        xv = wk(12 * 128).rearrange("p (u c) -> p u c", u=12)
        gg = wk(12 * 128).rearrange("p (u c) -> p u c", u=12)
        scr = [work[:, inv0 + i * TP:inv0 + (i + 1) * TP] for i in range(11)]
        assert 11 * TP <= 36 * 128
        sg, aa = scr[0:2], scr[2:4]
        Ls, Lx, Pc, Pi, Px, kd, tb = scr[4:11]
        rest = [inv0 + 12 * 128]

        def again(n):
            rest[0] += n
            assert rest[0] <= at[0]
            return work[:, rest[0] - n:rest[0]]

        sdp = again(2 * 640).rearrange("p (h c) -> p h c", h=2)
        ropet = sdp.rearrange("p h c -> p (h c)")[:, 0:512].rearrange("p (k t) -> p k t", k=2)
        qx = again(512).rearrange("p (d t) -> p d t", d=2)
        xi = again(512).rearrange("p (d t) -> p d t", d=2)
        ysq_r = sdp.rearrange("p h c -> p (h c)")[:, 384:384 + TP]
        rroot = sdp.rearrange("p h c -> p (h c)")[:, 384 + TP:384 + 2 * TP]
        yb, yc, ysq, yroot = scr[4:8]
        scores = [again(384), sdp.rearrange("p h c -> p (h c)")[:, 0:384]]
        ptr = again(384).rearrange("p (k q) -> p k q", k=3)
        wact = [work[:, i * TP:(i + 1) * TP] for i in range(FT)]
        o = FT * TP
        merged = [work[:, o + i * TP:o + (i + 1) * TP] for i in range(KT)]
        o += KT * TP
        ybuf = [work[:, o + i * TP:o + (i + 1) * TP] for i in range(KT)]
        o += KT * TP
        ctmp = [work[:, o + i * TP:o + (i + 1) * TP] for i in range(8)]
        sq = [ctmp[6], ctmp[7]]
        o += 8 * TP
        rstd = work[:, o:o + TP]
        o += TP
        assert o <= WORK, o

        handles = []

        def sem(name):
            s = ctx.enter_context(nc.semaphore(name))
            handles.append(s)
            return Signal(s)

        setup = ctx.enter_context(nc.semaphore("setup"))
        w_loaded = [sem(f"w_loaded{i}") for i in range(RING)]
        
        names = """
            a_step act_ready ada_done au_done au_ready bias_ready bon_done bon_used
            bt_done bt_ready c_ready cg_done cg_ready cn_decay cn_done cn_ready
            cu_done cu_ready de_ready dt_ready exp_ready g0_done g0_ready gelu_ready
            gl_done gl_ready gn_done h_ready hnorm kd_ready kk_ready kk_rk kk_sq
            kkn_done kkn_root kt_done kt_ready la_done lora_in lp_exp lw_done
            lx_ready mod_ready mrg_ready mx_ready no_done no_ready o_ready out_k
            out_st p_ready p_step pend_ready pk_in pn_ready prm_in pt_done pt_ready
            qx_ready rgn_done ro_ready rope_done rope_ready rr_ready rroot_ready
            rsq_ready rst_done rst_ready rt_root ry_done ry_ready ryc_ready s_ready
            sc_done scan_ready sctx_ready sd_ready sig_ready silu_c sq_ready sq_used
            ss_done st0_ready st_done til_ready tr_done v_step vt_done vt_ready
            w_used x_init x_ready x_upd xi_ready xt_done y_copied y_done yc_ready
            yroot_ready ysq_ready z_done zr_ready""".split()
        S = {n: sem(n) for n in names}
        z_free = [sem("z_free0").h, sem("z_free1").h]

        with nc.Block() as block:
            @block.sync
            def _(sp):
                sp.dma_start(const[:, :], const_d).then_inc(setup, 16)
                sp.dma_start(xres[:, :], xin).then_inc(setup, 16)
                sp.dma_start(cc[:, :], cc_d).then_inc(setup, 16)
                sp.wait_ge(setup, 48 + 5)

            @block.vector
            def _(dve):
                dve.memset(hbuf[:, :], 0.0).then_inc(setup, 1)
                dve.memset(mix[:, :], 0.0).then_inc(setup, 1)
                dve.memset(eps_rms, 1e-6).then_inc(setup, 1)
                dve.memset(eps_rw, 64e-5).then_inc(setup, 1)
                dve.memset(eps_rt, 1e-5).then_inc(setup, 1)

        with nc.Fori(0, DEPTH) as layer:
            with nc.Block() as block:
                ZP, ZM = 2, 2 + 11 * PAIRS
                ZO = ZM + 6 * KT
                ZU = ZO + KT
                ZD = ZU + 2 * FT

                def unit(tt, d, hb):
                    return 4 * tt + 2 * d + hb

                def z(zi, n=TP):
                    return psz[:, zi % 2, 0:n]

                def w(b, a=0, n=TP):
                    return psw[:, b, a:a + n]

                def rows(hb):
                    return slice(64 * hb, 64 * hb + 64)

                def place(s, n, d):
                    if s == 0:
                        j = n if d == 0 else 3 - n
                        return 1 + j // 2, CH * (j % 2), 2 + j
                    j = n if d == 0 else 1 - n
                    return 0, CH * j, j

                def step_of(tt, half, d):
                    if tt == 0:
                        return half if d == 0 else 1 - half
                    j = 2 * (tt - 1) + half
                    return 2 + (j if d == 0 else 3 - j)

                JOBS = [(hb, kind) for hb in range(2) for kind in range(3)]

                @block.sync
                def _(sp):
                    sp.dma_start(prm[:, :], prm_d[layer]).then_inc(S["prm_in"].h, 16)
                    for b in range(RING):
                        sp.dma_start(ring[:, b * 1024:(b + 1) * 1024], wstream[layer, b]).then_inc(w_loaded[b].h, 16)
                    with sp.Fori(1, BLOCKS // RING) as i:
                        for b in range(RING):
                            sp.wait_ge(S["w_used"].h, i * RING + (b - RING + 1))
                            sp.dma_start(ring[:, b * 1024:(b + 1) * 1024], wstream[layer, i * RING + b]).then_inc(w_loaded[b].h, 16)
                    for b in range(BLOCKS // RING * RING, BLOCKS):
                        sp.wait_ge(S["w_used"].h, b - RING + 1)
                        s = b % RING
                        sp.dma_start(ring[:, s * 1024:(s + 1) * 1024], wstream[layer, b]).then_inc(w_loaded[s].h, 16)

                @block.tensor
                def _(pe):
                    used = [0]

                    def mm(out, a, b, start=True, stop=True, sig=None):
                        ins = nc.tensor.matmul(out, a, b, start=start, stop=stop, skip_group_check=True)
                        if sig:
                            S[sig].by(ins)
                        elif used[0]:
                            S["w_used"].by(ins, used[0])
                            used[0] = 0

                    def tr(out, a, sig=None):
                        ins = nc.tensor.transpose(out, a, ident)
                        if sig:
                            S[sig].by(ins)

                    def loaded(b):
                        pe.wait_ge(w_loaded[b % RING].h, 16 * (b // RING + 1))
                        return slot[b % RING]

                    def opened(zi):
                        if zi >= 2:
                            pe.wait_ge(z_free[zi % 2], zi // 2)
                        return z(zi)

                    def dense(zi, b, src=h):
                        out, wt = opened(zi), loaded(b)
                        for k in range(KT):
                            mm(out, wt[:, k, :], src[k], k == 0, k == KT - 1, "z_done" if k == KT - 1 else None)
                        used[0] += 1

                    def dense_rows(zi, b):
                        opened(zi)
                        wt = loaded(b)
                        for t in range(3):
                            for k in range(KT):
                                mm(psz[:, zi % 2, t * P:(t + 1) * P], h[k][:, TT[t]:TT[t] + P], wt[:, k, :], k == 0,
                                   k == KT - 1, "z_done" if (t, k) == (2, KT - 1) else None)
                        used[0] += 1

                    def sum_squares(j):
                        for k in range(KT):
                            pe.wait_ge(S["sq_ready"].h, KT * j + k + 1)
                            mm(w(0), ones, sq[k % 2], k == 0, k == KT - 1, "ss_done" if k == KT - 1 else "sq_used")

                    sum_squares(0)
                    pe.wait_ge(S["silu_c"].h, 1)
                    for m in range(48):
                        wt = loaded(ADA0 + m)
                        for k in range(KT):
                            mm(psw[:, 1, 2 * m:2 * m + 2], wt[:, k, :], cs[:, k, :], k == 0, k == KT - 1,
                               "ada_done" if (m, k) == (47, KT - 1) else None)
                        used[0] += 1
                    pe.wait_ge(S["h_ready"].h, 2 * KT)
                    dense(0, SHARED0)
                    dense(1, SHARED0 + 1)

                    for p in range(PAIRS):
                        zb, bb = ZP + 11 * p, PAIR0 + 10 * p
                        for i in range(5):
                            dense(zb + i, bb + i)
                        dense_rows(zb + 5, bb + 5)
                        if p:
                            pe.wait_ge(S["o_ready"].h, p)
                            pe.wait_ge(S["no_ready"].h, 2 * p)
                            pe.wait_ge(S["ro_ready"].h, p)
                        pe.wait_ge(S["kk_sq"].h, p + 1)
                        mm(w(0), blk, tb, sig="kkn_done")
                        pe.wait_ge(S["kk_rk"].h, p + 1)
                        mm(w(1), blk, kd, sig="bon_done")
                        pe.wait_ge(S["pk_in"].h, 16 * (p + 1))
                        pe.wait_ge(S["lora_in"].h, 2)
                        lora = pk[:, PK["lora"]:PK["lora"] + 256]
                        for d in range(2):
                            mm(w(2 + d), lora[0:64, d * P:(d + 1) * P], lwal[0:64, :], sig="lw_done")
                        for d in range(2):
                            mm(w(4 + d), lora[64:128, d * P:(d + 1) * P], lwal[64:128, :], sig="la_done")
                        mm(opened(zb + 6), pk[:, PK["g_up"]:PK["g_up"] + P], lgl, sig="z_done")
                        dense(zb + 7, bb + 6)
                        dense(zb + 8, bb + 7)
                        dense_rows(zb + 9, bb + 8)
                        dense(zb + 10, bb + 9)

                        pe.wait_ge(S["kkn_root"].h, p + 1)
                        for t in range(3):
                            tr(w(0, t * P, P), vc[:, TT[t]:TT[t] + P], "vt_done" if t == 2 else None)
                        pe.wait_ge(S["bon_used"].h, p + 1)
                        pe.wait_ge(S["sig_ready"].h, 4 * p + 4)
                        for d in range(2):
                            pe.wait_ge(S["til_ready"].h, 2 * p + d + 1)
                            for k in range(2):
                                for t in range(3):
                                    tr(w(1 + 2 * d + k, t * P, P), bk[:, d, k, TT[t]:TT[t] + P],
                                       "bt_done" if t == 2 else None)
                        pe.wait_ge(S["rr_ready"].h, 2 * p + 2)
                        for u in range(12):
                            t, d, hb = u // 4, u // 2 % 2, u % 2
                            b, c, r = u % 6, slice(TT[t], TT[t] + P), rows(hb)
                            if u == 0:
                                pe.wait_ge(S["vt_ready"].h, p + 1)
                            elif u < 5:
                                pe.wait_ge(S["bt_ready"].h, 4 * p + u)
                            elif u >= 6:
                                pe.wait_ge(S["au_ready"].h, 12 * p + u - 5)
                            for k in range(2):
                                mm(w(b, 256 * k, 256).rearrange("p (k c) -> p k c", k=2), bk[r, d, k, c], ar[r, d, :, c],
                                   sig="au_done" if k else None)
                        for g in range(3):
                            pe.wait_ge(S["au_ready"].h, 12 * p + max(4 * g + 4, g + 7))
                            for i in range(4):
                                tr(w(g, i * P, P), au[:, 4 * g + i, 0, :], "tr_done" if i == 3 else None)
                        for d in range(2):
                            for t in range(3):
                                for hb in range(2):
                                    mm(w(3 + d, t * P + 64 * hb, 64), au[:, unit(t, d, hb), 2, :],
                                       vt[:, t, rows(hb)], sig="g0_done" if (t, hb) == (2, 1) else None)
                        i = 0
                        for lv in range(1, LEVELS):
                            for g in range(3):
                                pe.wait_ge(S["x_ready"].h, 33 * p + 6 * (lv - 1) + 2 * g + 2)
                                for q in range(4):
                                    mm(w(g, q * P, P), au[:, 4 * g + q, 0, :], xv[:, 4 * g + q, :],
                                       sig="gl_done" if q == 3 else None)
                            for g in range(3):
                                pe.wait_ge(S["gl_ready"].h, 15 * p + 3 * (lv - 1) + g + 1)
                                for side in range(1 if lv == LEVELS - 1 else 0, 2):
                                    if i >= 3:
                                        pe.wait_ge(S["x_ready"].h, 33 * p + 6 + i - 2)
                                    elif i < 2:
                                        pe.wait_ge(S["g0_ready"].h, 2 * p + i + 1)
                                    for q in range(4):
                                        u = 4 * g + q
                                        a, b = (gg, tvv) if side else (tvv, gg)
                                        mm(w(3 + i % 3, q * P, P), a[:, u, :], b[:, u, :],
                                           sig="xt_done" if q == 3 else None)
                                    i += 1

                        pe.wait_ge(S["x_ready"].h, 33 * (p + 1))
                        pe.wait_ge(S["g0_ready"].h, 2 * p + 2)

                        def scores_mm(j):
                            hb, kind = JOBS[j]
                            q = nq[rows(hb), TT[kind]:TT[kind] + P]
                            if j == 0:
                                pe.wait_ge(S["ry_ready"].h, 2 * (p + 1))
                            else:
                                pe.wait_ge(S["s_ready"].h, 6 * p + j)
                            if kind == 0:
                                mm(w(4, 0, P), q, nk[rows(hb), 0:P], sig="sc_done")
                            else:
                                mm(w(4, 0, P), q, pk[rows(hb), PK["kc"]:PK["kc"] + P])
                                mm(w(4, P, 256), q, nk[rows(hb), LAT:TP], sig="sc_done")

                        def values_mm(j):
                            hb, kind = JOBS[j]
                            n = 3 if kind else 1
                            pe.wait_ge(S["pn_ready"].h, 6 * p + j + 1)
                            if j == 0:
                                pe.wait_ge(S["rst_ready"].h, 4 * (p + 1))
                            for i in range(n):
                                tr(w(5, i * P, P), scores[j % 2][:, i * P:(i + 1) * P], "pt_done" if i == n - 1 else None)
                            pe.wait_ge(S["pt_ready"].h, 6 * p + j + 1)
                            for i in range(n):
                                v = nv[:, i, rows(hb)]
                                if kind and i == 0:
                                    v = pk[:, PK["vc"] + 64 * hb:PK["vc"] + 64 * hb + 64]
                                mm(psw[rows(hb), 3, kind * P:(kind + 1) * P], v, ptr[:, i, :], i == 0, i == n - 1,
                                   "no_done" if i == n - 1 else None)

                        def fill(i):
                            if i == 0:
                                mm(w(4, 0, 256), perm, tq[:, LAT:TP])
                                mm(w(4, 256, 256), perm, tk[:, LAT:TP], sig="rope_done")
                                tr(w(5, 0, P), tk[:, 0:P], "kt_done")
                            elif i in (1, 2):
                                r = rows(i - 1)
                                if i == 1:
                                    pe.wait_ge(S["rope_ready"].h, 2 * (p + 1))
                                    pe.wait_ge(S["kt_ready"].h, 4 * (p + 1))
                                else:
                                    pe.wait_ge(S["sd_ready"].h, 4 * p + 2)
                                mm(w(4, 0, P), tk[r, 0:P], tq[r, 0:P])
                                mm(w(4, P, 256), tk[r, TT[1]:TT[1] + P], tq[r, LAT:TP], sig="st_done")
                                mm(w(5, 0, 256), tk[r, TT[2]:TT[2] + P], tq[r, LAT:TP], sig="st_done")
                            elif i == 3:
                                pe.wait_ge(S["sd_ready"].h, 4 * (p + 1))
                                for hb in range(2):
                                    mm(psw[rows(hb), 4, 0:P], tv[:, 0, rows(hb)], sdp[:, hb, 0:P], True, False)
                                    for t in range(2):
                                        mm(psw[rows(hb), 4, P:3 * P], tv[:, 1 + t, rows(hb)],
                                           sdp[:, hb, P + 256 * t:P + 256 * t + 256], False, False)
                                pe.wait_ge(S["qx_ready"].h, 2 * (p + 1))
                                pe.wait_ge(S["st0_ready"].h, 8 * (p + 1))
                                for d in range(2):
                                    mm(w(4, P, 256), s0[:, d, :], qx[:, d, :], False, d == 1, "ry_done" if d else None)
                                for d in range(2):
                                    mm(w(5, d * P, P), ktz[:, d, :], tv[:, 0, :], sig="rst_done" if d else None)
                            elif i < 11:
                                if i < 10:
                                    scores_mm(i - 4)
                                if i > 4:
                                    values_mm(i - 5)
                            elif i == 11:
                                pe.wait_ge(S["s_ready"].h, 6 * (p + 1))
                                mm(w(4), blk, tq, sig="rgn_done")
                                pe.wait_ge(S["rsq_ready"].h, p + 1)
                                pe.wait_ge(S["pt_ready"].h, 6 * (p + 1))
                                mm(w(5), blk, ysq_r, sig="rgn_done")

                        slot_i = 0
                        for n in range(4):
                            strm = (0, 1) if n < 2 else (0,)
                            pe.wait_ge(S["cn_ready"].h, CN_PAIR * p + (0, 8, 16, 20)[n]) if CN_PAIR * p + n else None
                            if n == 0:
                                pe.wait_ge(S["st0_ready"].h, 8 * (p + 1))
                            for s in strm:
                                for d in range(2):
                                    t, cb, _ = place(s, n, d)
                                    c = (2 + n) if s == 0 else n
                                    mm(psw[cb:cb + 64, 0, 256 * s:256 * s + P], ar[:, d, 0, TT[t] + cb:TT[t] + cb + 64],
                                       st[:, d, c, :], sig="cg_done" if d else None)
                            fill(slot_i)
                            pe.wait_ge(S["cg_ready"].h, 12 * p + (4, 8, 10, 12)[n])
                            for s in strm:
                                for d in range(2):
                                    t, cb, _ = place(s, n, d)
                                    for hb in range(2):
                                        mm(psw[cb:cb + 64, 0, 256 * s + P + 64 * hb:256 * s + P + 64 * hb + 64],
                                           tvv[cb:cb + 64, unit(t, d, hb), cb:cb + 64], gs[cb:cb + 64, s, rows(hb)],
                                           sig="cu_done" if d and hb else None)
                            fill(slot_i + 1)
                            pe.wait_ge(S["cu_ready"].h, 12 * p + (4, 8, 10, 12)[n])
                            for s in strm:
                                if n == 3:
                                    break
                                for d in range(2):
                                    t, cb, _ = place(s, n, d)
                                    o_ = psw[:, 1 + d, s * P:s * P + P]
                                    mm(o_, bkt[cb:cb + 64, d, 0, t, :], ut[cb:cb + 64, d, t, :], True, False)
                                    mm(o_, bkt[cb:cb + 64, d, 1, t, :], vt[cb:cb + 64, t, :], False, True,
                                       "cn_done" if d else None)
                            fill(slot_i + 2)
                            slot_i += 3

                        for t in range(3):
                            for d in range(2):
                                for hb in range(2):
                                    u, o_ = unit(t, d, hb), psw[rows(hb), 0, t * P:(t + 1) * P]
                                    mm(o_, vt[:, t, rows(hb)], au[:, u, 3, :], t == 0 and d == 0, False)
                                    mm(o_, ut[:, d, t, rows(hb)], au[:, u, 1, :], False, False)
                                for half in range(2):
                                    a = TT[t] + CH * half
                                    mm(w(0, t * P + CH * half, CH), st[:, d, step_of(t, half, d), :], ar[:, d, 1, a:a + CH],
                                       False, (t, d, half) == (2, 1, 1), "y_done" if (t, d, half) == (2, 1, 1) else None)
                        pe.wait_ge(S["y_copied"].h, 2 * (p + 1))
                        mm(w(1), blk, yb, sig="gn_done")
                        pe.wait_ge(S["ysq_ready"].h, p + 1)
                        mm(w(2), blk, ysq, sig="gn_done")

                    for b in range(3):
                        pe.wait_ge(S[("o_ready", "no_ready", "ro_ready")[b]].h, (1, 2, 1)[b] * PAIRS)
                    for m in range(KT):
                        base = MERGE0 + 9 * (m // 2)
                        gate_blocks = (base, base + 2, base + 3) if m % 2 == 0 else (base + 5, base + 6, base + 8)
                        for b in range(3):
                            dense(ZM + 6 * m + 2 * b, gate_blocks[b])
                            joint = b == 1 if m % 2 == 0 else b != 1
                            if joint:
                                used[0] -= 1
                            zi = ZM + 6 * m + 2 * b + 1
                            out = opened(zi)
                            for k in range(PAIRS):
                                un = 12 * (m % 2) + 4 * b + k
                                wb = base + (1, 4, 7)[un // 8]
                                wt = loaded(wb)
                                mm(out, wt[:, un % 8, :], mixed[b][k], k == 0, k == PAIRS - 1,
                                   "z_done" if k == PAIRS - 1 else None)
                            used[0] += 2 if joint else 0
                    pe.wait_ge(S["mrg_ready"].h, KT)
                    for m in range(KT):
                        dense(ZO + m, OUT0 + m, merged)
                        if m:
                            pe.wait_ge(S["sq_ready"].h, KT + m)
                            mm(w(0), ones, sq[(m - 1) % 2], m == 1, False, "sq_used")
                    pe.wait_ge(S["sq_ready"].h, 2 * KT)
                    mm(w(0), ones, sq[(KT - 1) % 2], False, True, "ss_done")
                    sum_squares(2)
                    pe.wait_ge(S["h_ready"].h, 4 * KT)
                    for i in range(2 * FT):
                        dense(ZU + i, UP0 + i)
                    pe.wait_ge(S["act_ready"].h, FT)
                    for m in range(KT):
                        out = opened(ZD + m)
                        for k in range(FT):
                            un = FT * m + k
                            wt = loaded(DOWN0 + un // 8)
                            mm(out, wt[:, un % 8, :], wact[k], k == 0, k == FT - 1, "z_done" if k == FT - 1 else None)
                            if un % 8 == 7:
                                used[0] += 1
                        if m:
                            pe.wait_ge(S["sq_ready"].h, 3 * KT + m)
                            mm(w(0), ones, sq[(m - 1) % 2], m == 1, False, "sq_used")
                    pe.wait_ge(S["sq_ready"].h, 4 * KT)
                    mm(w(0), ones, sq[(KT - 1) % 2], False, True, "ss_done")

                @block.scalar
                def _(act):
                    L = Lane(act, S["a_step"], z_free)

                    def run(out, src, f=ACT.Copy, sig=None, free=None, **kw):
                        L.do(nc.scalar.activation(out, src, f, **kw), S[sig] if sig else None, free)

                    def seen(zi):
                        act.wait_ge(S["z_done"].h, zi + 1)

                    def square_out(src, k, j):
                        if k >= 2:
                            act.wait_ge(S["sq_used"].h, (KT - 1) * j + k - 1)
                        elif j:
                            act.wait_ge(S["ss_done"].h, j)
                        run(sq[k % 2], src, ACT.Square, "sq_ready")

                    def root(j):
                        act.wait_ge(S["ss_done"].h, j + 1)
                        run(rstd, w(0), ACT.Sqrt, "rt_root", scale=1.0 / D, bias=eps_rms)

                    def modulate(j, scale, shift):
                        for k in range(KT):
                            act.wait_ge(S["hnorm"].h, KT * j + k + 1)
                            for s, _, a, b in STREAMS:
                                run(h[k][:, a:b], h[k][:, a:b], ACT.Identity, "h_ready",
                                    scale=scale[:, k, s:s + 1], bias=mod[:, shift + k, s:s + 1])

                    run(cs, cc[:, :].rearrange("p (k s) -> p k s", s=2), ACT.Silu, "silu_c")
                    for k in range(KT):
                        square_out(x[k], k, 0)
                    root(0)
                    act.wait_ge(S["prm_in"].h, 16)
                    run(lt, prm[:, PRM["dec_ch"]:PRM["dec_ch"] + 24], ACT.Abs)
                    L.settle()
                    run(lt, lt, ACT.Exp, "lp_exp", scale=-1.0)
                    act.wait_ge(S["mod_ready"].h, 1)
                    modulate(0, scale1, 0)

                    def centre_tap(dst, zi, name, tile):
                        seen(zi)
                        run(dst, z(zi), ACT.Identity, "c_ready", scale=par(name, 3 * tile + 1), bias=0.0)

                    centre_tap(lwal, 0, "conv", 12)
                    centre_tap(lgl, 1, "conv", 13)
                    act.wait_ge(z_free[0], 1)
                    run(lwal[0:64, :], lwal[0:64, :], ACT.Tanh, "lora_in")
                    act.wait_ge(z_free[1], 1)
                    run(lgl, lgl, ACT.Sigmoid, "lora_in")

                    def load_pack(p):
                        act.dma_start(pk[:, :], pk_d[layer, p]).then_inc(S["pk_in"].h, 16)

                    load_pack(0)
                    for p in range(PAIRS):
                        zb = ZP + 11 * p
                        if p:
                            act.wait_ge(S["til_ready"].h, 2 * p)
                            act.wait_ge(S["rr_ready"].h, 2 * p)
                        for i, dst in enumerate((rc, kc_, vc)):
                            centre_tap(dst, zb + i, "conv", 4 * i + p)
                        seen(zb + 3)
                        run(nq, z(zb + 3), free=zb + 3, scale=0.125)
                        seen(zb + 4)
                        if p:
                            act.wait_ge(S["out_k"].h, 32 * p)
                        run(nk, z(zb + 4), free=zb + 4)
                        seen(zb + 5)
                        run(nv, z(zb + 5, 384).rearrange("p (t c) -> p t c", t=3), free=zb + 5)
                        L.settle()
                        act.wait_ge(z_free[zb % 2], (zb + 4) // 2 + 1)
                        act.dma_start(nak[layer, p], nk[:, 0:P]).then_inc(S["out_k"].h, 16)
                        act.dma_start(nav[layer, p], nv[:, 0, :]).then_inc(S["out_k"].h, 16)
                        if p:
                            act.wait_ge(S["o_ready"].h, p)
                            act.wait_ge(S["ro_ready"].h, p)
                        act.wait_ge(S["kkn_done"].h, p + 1)
                        run(Pi, w(0), ACT.Sqrt, "kkn_root")
                        for d in range(2):
                            act.wait_ge(S["lw_done"].h, 2 * p + d + 1)
                            run(sg[d], w(2 + d), ACT.Sigmoid, "sig_ready", bias=par("w0", 4 * d + p))
                        for d in range(2):
                            act.wait_ge(S["la_done"].h, 2 * p + d + 1)
                            run(aa[d], w(4 + d), ACT.Sigmoid, "sig_ready", bias=par("a0", 4 * d + p))
                        seen(zb + 6)
                        run(gr, z(zb + 6), free=zb + 6)
                        seen(zb + 7)
                        run(tq, z(zb + 7), free=zb + 7)
                        seen(zb + 8)
                        run(tk, z(zb + 8), free=zb + 8, scale=0.125)
                        act.wait_ge(S["kk_ready"].h, p + 1)
                        for d in range(2):
                            if d:
                                act.wait_ge(S["til_ready"].h, 2 * p + 1)
                                act.wait_ge(S["rr_ready"].h, 2 * p + 1)
                            act.wait_ge(S["scan_ready"].h, 2 * p + d + 1)
                            run(Pi, Ls, ACT.Exp, "exp_ready", scale=DECAY_C)
                            run(Pc, Ls, ACT.Exp, "exp_ready", scale=-DECAY_C)
                            act.wait_ge(S["lx_ready"].h, 2 * p + d + 1)
                            run(Px, Lx, ACT.Exp, "exp_ready", scale=-DECAY_C)
                            if d == 0:
                                seen(zb + 9)
                                run(tv, z(zb + 9, 384).rearrange("p (t c) -> p t c", t=3), free=zb + 9)
                                seen(zb + 10)
                                run(tg, z(zb + 10), ACT.Silu, free=zb + 10)
                        act.wait_ge(S["vt_done"].h, p + 1)
                        run(vt, w(0, 0, 384).rearrange("p (t c) -> p t c", t=3), sig="vt_ready")
                        for d in range(2):
                            for k in range(2):
                                act.wait_ge(S["bt_done"].h, 4 * p + 2 * d + k + 1)
                                run(bkt[:, d, k], w(1 + 2 * d + k, 0, 384).rearrange("p (t c) -> p t c", t=3), sig="bt_ready")
                        for d in range(2):
                            for hb in range(2):
                                r = rows(hb)
                                run(st[r, d, 2, r], pk[r, PK["s_rw"] + 64 * d:PK["s_rw"] + 64 * d + 64], sig="st0_ready")
                                run(s0[r, d, r], pk[r, PK["s_rt"] + 64 * d:PK["s_rt"] + 64 * d + 64], sig="st0_ready")
                        for d in range(2):
                            act.wait_ge(S["g0_done"].h, 2 * p + d + 1)
                            run(g0[:, d], w(3 + d, 0, 384).rearrange("p (t c) -> p t c", t=3), sig="g0_ready")
                        for lv in range(1, LEVELS):
                            for g in range(3):
                                act.wait_ge(S["gl_done"].h, 15 * p + 3 * (lv - 1) + g + 1)
                                run(gg[:, 4 * g:4 * g + 4, :], w(g, 0, 512).rearrange("p (u c) -> p u c", u=4), sig="gl_ready")
                            if lv == 1:
                                for hb in range(2):
                                    act.wait_ge(S["dt_ready"].h, 2 * p + hb + 1)
                                    run(dtab[:, hb, :], dtab[:, hb, :], ACT.Exp, "de_ready")
                                for d in range(2):
                                    for hb in range(2):
                                        i = 8 + 8 * d + 2 * p + hb
                                        run(zeta[:, 2 * d + hb:2 * d + hb + 1], cv("zp", 1, d), ACT.Exp,
                                            scale=lg[:, i:i + 1])
                        act.wait_ge(S["xt_done"].h, 27 * (p + 1))

                        def scores_act(j):
                            hb, kind = JOBS[j]
                            act.wait_ge(S["sc_done"].h, 6 * p + j + 1)
                            if j >= 2:
                                act.wait_ge(S["pt_done"].h, 6 * p + j - 1)
                            run(scores[j % 2][:, 0:P], w(4, 0, P), sig="sctx_ready")

                        def probs_t(j):
                            n = 3 if JOBS[j][1] else 1
                            act.wait_ge(S["pt_done"].h, 6 * p + j + 1)
                            if j:
                                act.wait_ge(S["no_done"].h, 6 * p + j)
                            run(ptr[:, 0:n, :], w(5, 0, n * P).rearrange("p (k q) -> p k q", k=n), sig="pt_ready")

                        def exps(j):
                            n = 384 if JOBS[j][1] else P
                            act.wait_ge(S["mx_ready"].h, 6 * p + j + 1)
                            s_ = scores[j % 2][:, 0:n]
                            run(s_, s_, ACT.Exp, "p_ready", bias=mx[:, j % 2:j % 2 + 1], accum_out=rs[:, j % 2:j % 2 + 1])

                        def fill(i):
                            if i == 0:
                                for d in range(2):
                                    if d == 0:
                                        act.wait_ge(S["kt_done"].h, p + 1)
                                        L.settle()
                                    for hb in range(2):
                                        run(ktz[:, d, rows(hb)], w(5, 64 * hb, 64), ACT.Copy, "kt_ready",
                                            scale=zeta[:, 2 * d + hb:2 * d + hb + 1])
                                for d in range(2):
                                    run(xi[:, d, :], cv("xi", 256, 256 * d), ACT.Exp, "xi_ready",
                                        scale=lg[:, 4 * d + p:4 * d + p + 1])
                            elif i == 3:
                                act.wait_ge(S["ry_done"].h, p + 1)
                                run(tq[:, 0:P], w(4, 0, P), sig="ry_ready")
                                run(tq[:, LAT:TP], w(4, P, 256), sig="ry_ready")
                                act.wait_ge(S["rst_done"].h, p + 1)
                                if p:
                                    act.wait_ge(S["out_st"].h, 32 * p)
                                for d in range(2):
                                    for hb in range(2):
                                        run(srtb[rows(hb), d, :], psw[rows(hb), 5, d * P + 64 * hb:d * P + 64 * hb + 64],
                                            sig="rst_ready")
                                L.settle()
                                act.dma_start(srt[layer, p], srtb.rearrange("p d v -> p (d v)")).then_inc(S["out_st"].h, 16)
                            elif 4 <= i < 11:
                                if i < 10:
                                    scores_act(i - 4)
                                if i > 4:
                                    probs_t(i - 5)
                                if i < 10:
                                    exps(i - 4)
                            elif i == 11:
                                act.wait_ge(S["no_done"].h, 6 * (p + 1))
                                run(mixed[1][p][:, 0:P], w(3, 0, P), sig="no_ready")
                                run(mixed[1][p][:, LAT:TP], w(3, P, 256), sig="no_ready")
                                act.wait_ge(S["ryc_ready"].h, p + 1)
                                run(ysq_r, tk, ACT.Square, "rsq_ready")
                                act.wait_ge(S["rgn_done"].h, 2 * (p + 1))
                                run(rroot, w(5), ACT.Sqrt, "rroot_ready", scale=1.0 / 64, bias=eps_rt)

                        slot_i = 0
                        for n in range(4):
                            strm = (0, 1) if n < 2 else (0,)
                            if n == 0:
                                act.wait_ge(S["pend_ready"].h, 4 * (p + 1))
                                L.settle()
                            for k, s in enumerate(strm):
                                if n == 3:
                                    break
                                if n:
                                    act.wait_ge(S["cn_ready"].h, CN_PAIR * p + (0, 4, 12, 20)[n] + 4 * k)
                                for d in range(2):
                                    _, _, c = place(s, n, d)
                                    run(stp[:, s, d, :], st[:, d, (2 + n) if s == 0 else n, :], ACT.Copy, "cn_decay",
                                        scale=pend[:, d, c:c + 1])
                            fill(slot_i)
                            act.wait_ge(S["cu_done"].h, 6 * p + (2, 4, 5, 6)[n])
                            for s in strm:
                                for d in range(2):
                                    t, cb, _ = place(s, n, d)
                                    run(ut[cb:cb + 64, d, t, :], psw[cb:cb + 64, 0, 256 * s + P:256 * s + 2 * P], sig="cu_ready")
                            fill(slot_i + 1)
                            fill(slot_i + 2)
                            slot_i += 3
                        act.wait_ge(S["cn_ready"].h, CN_PAIR * p + 16)
                        act.dma_start(srw[layer, p], fin.rearrange("p d v -> p (d v)")).then_inc(S["out_st"].h, 16)
                        act.wait_ge(S["y_done"].h, p + 1)
                        run(yb[:, 0:P], w(0, 0, P), sig="y_copied")
                        run(yb[:, LAT:TP], w(0, P, 256), sig="y_copied")
                        act.wait_ge(S["yc_ready"].h, p + 1)
                        run(ysq, yc, ACT.Square, "ysq_ready")
                        act.wait_ge(S["gn_done"].h, 2 * (p + 1))
                        run(yroot, w(2), ACT.Sqrt, "yroot_ready", scale=1.0 / 64, bias=eps_rw)
                        if p + 1 < PAIRS:
                            act.wait_ge(S["s_ready"].h, 6 * (p + 1))
                            load_pack(p + 1)

                    act.wait_ge(S["o_ready"].h, PAIRS)
                    for m in range(KT):
                        for b in range(3):
                            zi = ZM + 6 * m + 2 * b
                            seen(zi)
                            if m:
                                act.wait_ge(S["mrg_ready"].h, m)
                            run(ctmp[b], z(zi), ACT.Sigmoid, free=zi)
                    for m in range(KT):
                        seen(ZO + m)
                        square_out(z(ZO + m), m, 1)
                        run(ybuf[m], z(ZO + m), free=ZO + m)
                    root(1)
                    for k in range(KT):
                        act.wait_ge(S["x_upd"].h, k + 1)
                        square_out(x[k], k, 2)
                    root(2)
                    modulate(1, scale2, 24)

                    for i in range(FT + 1):
                        if i < FT:
                            if i >= 2:
                                act.wait_ge(S["act_ready"].h, i - 1)
                            for v in range(2):
                                centre_tap(ctmp[2 * (i % 2) + v], ZU + 2 * i + v, "fconv", i + FT * v)
                        if i:
                            zi = ZU + 2 * i - 1
                            act.wait_ge(z_free[zi % 2], zi // 2 + 1)
                            g_ = ctmp[2 * ((i - 1) % 2) + 1]
                            run(g_, g_, ACT.Gelu_apprx_tanh, "gelu_ready")
                    for m in range(KT):
                        seen(ZD + m)
                        square_out(z(ZD + m), m, 3)
                        run(ybuf[m], z(ZD + m), free=ZD + m)
                    root(3)

                @block.vector
                def _(dve):
                    L = Lane(dve, S["v_step"], z_free)
                    V = nc.vector

                    def sig_of(sig, free):
                        return S[sig] if sig else None, free

                    def tt(out, a, b, op=ALU.mult, sig=None, free=None):
                        L.do(V.tensor_tensor(out, a, b, op), *sig_of(sig, free))

                    def ts(out, a, s1, s2=None, op0=ALU.mult, op1=ALU.bypass, sig=None):
                        L.do(V.tensor_scalar(out, a, s1, s2, op0, op1), *sig_of(sig, None))

                    def stt(out, a, s_, b, op0=ALU.mult, op1=ALU.mult, sig=None, free=None):
                        L.do(V.scalar_tensor_tensor(out, a, s_, b, op0, op1), *sig_of(sig, free))

                    def recip(out, a, sig=None):
                        L.do(V.reciprocal(out, a), *sig_of(sig, None))

                    def pred(out, mask, data, sig):
                        L.do(V.copy_predicated(out, mask, data), S[sig])

                    def normed(j):
                        for k in range(KT):
                            for s, _, a, b in STREAMS:
                                tt(h[k][:, a:b], x[k][:, a:b], rstd[:, a:b], sig="hnorm" if s else None)

                    def rstd_of(j):
                        dve.wait_ge(S["rt_root"].h, j + 1)
                        recip(rstd, rstd)
                        L.settle()

                    def residual(j, gate):
                        for k in range(KT):
                            tt(ybuf[k], ybuf[k], rstd)
                            L.settle()
                            for s, _, a, b in STREAMS:
                                stt(x[k][:, a:b], ybuf[k][:, a:b], gate[:, k, s:s + 1], x[k][:, a:b], op1=ALU.add,
                                    sig="x_upd" if s else None)

                    def taps(dst, zi, name, tile):
                        taps.n += 1
                        dve.wait_ge(S["c_ready"].h, taps.n)
                        zt = z(zi)
                        stt(dst[:, 1:TP], zt[:, 0:TP - 1], par(name, 3 * tile), dst[:, 1:TP], op1=ALU.add)
                        L.settle()
                        stt(dst[:, 0:TP - 1], zt[:, 1:TP], par(name, 3 * tile + 2), dst[:, 0:TP - 1], op1=ALU.add, free=zi)

                    taps.n = 0

                    dve.wait_ge(S["prm_in"].h, 16)
                    dec = prm[:, PRM["dec_ch"]:PRM["dec_ch"] + 24]
                    ts(omka, prm[:, PRM["k_a"]:PRM["k_a"] + 4], -1.0, 1.0, op1=ALU.add)
                    ts(lg, dec, 0.0, op0=ALU.min)
                    dve.wait_ge(S["lp_exp"].h, 1)
                    ts(ls, lt, 2.0, op0=ALU.add)
                    L.settle()
                    recip(ls, ls)
                    L.settle()
                    tt(ls, ls, lt)
                    L.settle()
                    tt(lt, ls, ls)
                    L.settle()
                    ts(lq, lt, 1.0 / 17)
                    for i in range(7, 0, -1):
                        L.settle()
                        stt(lq, lq, 1.0 / (2 * i + 1), lt, op0=ALU.add)
                    L.settle()
                    stt(lq, lq, 1.0, ls, op0=ALU.add)
                    L.settle()
                    stt(lg, lq, -2.0, lg, op1=ALU.add)
                    rstd_of(0)
                    normed(0)
                    dve.wait_ge(S["ada_done"].h, 1)
                    tt(mod, psw[:, 1, 0:96].rearrange("p (m s) -> p m s", s=2),
                       prm[:, PRM["ada_b"]:PRM["ada_b"] + 48].unsqueeze(2).to_broadcast([P, 48, 2]), ALU.add)
                    L.settle()

                    def both(name):
                        return prm[:, PRM[name]:PRM[name] + KT].unsqueeze(2).to_broadcast([P, KT, 2])

                    stt(scale2, mod[:, 32:40], 1.0, both("ffn_pre"), op0=ALU.add)
                    tt(gate1, mod[:, 16:24], both("mix_post"))
                    tt(gate2, mod[:, 40:48], both("ffn_post"))
                    stt(scale1, mod[:, 8:16], 1.0, both("mix_pre"), op0=ALU.add, sig="mod_ready")
                    taps(lwal, 0, "conv", 12)
                    taps(lgl, 1, "conv", 13)

                    def level_masks(lv):
                        m = cv("lev", 256, 256 * lv).bitcast(U32).rearrange("p (d c) -> p d c", d=2)
                        m0 = m.unsqueeze(2).to_broadcast([P, 2, 2, P])
                        m1 = m[:, ::-1, :].unsqueeze(2).to_broadcast([P, 2, 2, P])
                        return m0, m1

                    def four(a):
                        return a.rearrange("p (d q) c -> p d q c", d=2)

                    for p in range(PAIRS):
                        zb = ZP + 11 * p
                        for i, dst in enumerate((rc, kc_, vc)):
                            taps(dst, zb + i, "conv", 4 * i + p)
                        L.settle()
                        ts(kk, kc_, par("k_k", p))
                        stt(kd, rc, par("r_k", p), kc_, sig="kk_rk")
                        L.settle()
                        tt(tb, kk, kk, sig="kk_sq")
                        dve.wait_ge(S["bon_done"].h, p + 1)
                        tt(bonus, w(1), vc, sig="bon_used")
                        dve.wait_ge(S["kkn_root"].h, p + 1)
                        ts(Pi, Pi, 1e-12, op0=ALU.max)
                        L.settle()
                        recip(Pi, Pi)
                        L.settle()
                        tt(kk, kk, Pi, sig="kk_ready")
                        for d in range(2):
                            L.settle()
                            dve.wait_ge(S["sig_ready"].h, 4 * p + d + 1)
                            rst = cv("reset", TP, TP * d)
                            order = slice(None, None, -1) if d else slice(None)
                            L.do(V.tensor_tensor_scan(Ls[:, order], rst[:, order], sg[d][:, order], 0.0, ALU.mult, ALU.add),
                                 S["scan_ready"])
                            dve.wait_ge(S["sig_ready"].h, 4 * p + d + 3)
                            L.settle()
                            tt(tb, kk, aa[d])
                            dve.wait_ge(S["kd_ready"].h, 2 * p + d + 1)
                            tt(kd, kd, kc_)
                            L.settle()
                            dve.wait_ge(S["exp_ready"].h, 6 * p + 3 * d + 3)
                            stt(ar[:, d, 0, :], kk, -1.0, Px)
                            tt(bk[:, d, 1, :], kd, Pi)
                            tt(bk[:, d, 0, :], tb, Pi, sig="til_ready")
                        for u in range(12):
                            d = u // 2 % 2
                            dve.wait_ge(S["au_done"].h, 12 * p + u + 1)
                            tt(au[:, u].rearrange("p (k e) c -> p k (e c)", k=2),
                               w(u % 6, 0, 512).rearrange("p (k c) -> p k c", k=2),
                               cv("tri", 256, 256 * d).unsqueeze(1).to_broadcast([P, 2, 256]), sig="au_ready")
                        dve.wait_ge(S["x_init"].h, 2 * (p + 1))
                        m0, m1 = level_masks(0)
                        for g in range(3):
                            dve.wait_ge(S["tr_done"].h, 3 * p + g + 1)
                            us = slice(4 * g, 4 * g + 4)
                            pred(four(xv[:, us]), m0, w(g, 0, 512).rearrange("p (d q c) -> p d q c", d=2, q=2), "x_ready")
                            pred(four(tvv[:, us]), m1, four(au[:, us, 0, :]), "x_ready")
                        for hb in range(2):
                            i = 8 + 2 * p + hb
                            ts(dtab[:, hb, :], cv("posd", 384), lg[:, i:i + 1])
                            L.settle()
                            stt(dtab[:, hb, :], cv("negd", 384), lg[:, i + 8:i + 9], dtab[:, hb, :], op1=ALU.add, sig="dt_ready")
                        i = 0
                        for lv in range(1, LEVELS):
                            m0, m1 = level_masks(lv)
                            for g in range(3):
                                us = slice(4 * g, 4 * g + 4)
                                for side in range(1 if lv == LEVELS - 1 else 0, 2):
                                    dve.wait_ge(S["xt_done"].h, 27 * p + i + 1)
                                    pred(four((tvv if side else xv)[:, us]), m1 if side else m0,
                                         w(3 + i % 3, 0, 512).rearrange("p (d q c) -> p d q c", d=2, q=2), "x_ready")
                                    i += 1

                        def softmax(j):
                            hb, kind = JOBS[j]
                            s_ = scores[j % 2]
                            dve.wait_ge(S["sctx_ready"].h, 6 * p + j + 1)
                            if kind:
                                a = PK["bias"] + 384 * hb + (P if kind == 1 else 0)
                                if j == 1:
                                    dve.wait_ge(S["bias_ready"].h, p + 1)
                                tt(s_[:, P:384], w(4, P, 256), pk[:, a:a + 256], ALU.add)
                                L.settle()
                            n = 384 if kind else P
                            L.do(V.tensor_reduce(mt[:, 0:1], s_[:, 0:n], AX.X, ALU.max), S["s_ready"])
                            L.settle()
                            ts(mx[:, j % 2:j % 2 + 1], mt[:, 0:1], -1.0, sig="mx_ready")
                            dve.wait_ge(S["p_ready"].h, 6 * p + j + 1)
                            recip(ri[:, j % 2:j % 2 + 1], rs[:, j % 2:j % 2 + 1])
                            L.settle()
                            ts(s_[:, 0:n], s_[:, 0:n], ri[:, j % 2:j % 2 + 1], sig="pn_ready")

                        def fill(i):
                            if i == 0:
                                dve.wait_ge(S["de_ready"].h, 2 * (p + 1))
                                tt(dtab, dtab, cv("diag", 384).unsqueeze(1).to_broadcast([P, 2, 384]), ALU.add)
                                dve.wait_ge(S["rope_done"].h, p + 1)
                                tt(ropet, w(4, 0, 512).rearrange("p (k t) -> p k t", k=2),
                                   sinT.unsqueeze(1).to_broadcast([P, 2, 256]))
                                tt(tq[:, LAT:TP], tq[:, LAT:TP], cosT)
                                tt(tk[:, LAT:TP], tk[:, LAT:TP], cosT)
                                L.settle()
                                tt(tq[:, LAT:TP], tq[:, LAT:TP], ropet[:, 0], ALU.add, sig="rope_ready")
                                tt(tk[:, LAT:TP], tk[:, LAT:TP], ropet[:, 1], ALU.add, sig="rope_ready")
                            elif i in (1, 2):
                                hb = i - 1
                                dve.wait_ge(S["st_done"].h, 4 * p + 2 * hb + 1)
                                tt(sdp[:, hb, 0:P], w(4, 0, P), dtab[:, hb, P:2 * P])
                                tt(sdp[:, hb, P:384], w(4, P, 256), dtab[:, hb, P:384], sig="sd_ready")
                                dve.wait_ge(S["st_done"].h, 4 * p + 2 * hb + 2)
                                tt(sdp[:, hb, 384:640], w(5, 0, 256), dtab[:, hb, 0:256], sig="sd_ready")
                            elif 4 <= i < 10:
                                softmax(i - 4)
                            elif i == 11:
                                dve.wait_ge(S["rgn_done"].h, 2 * p + 1)
                                stt(tk, w(4), -1.0 / 64, tq, op1=ALU.add, sig="ryc_ready")
                                dve.wait_ge(S["rroot_ready"].h, p + 1)
                                recip(rroot, rroot)
                                L.settle()
                                tt(tk, tk, rroot)
                                L.settle()
                                stt(mixed[2][p], tk, par("gn", p), tg, sig="ro_ready")

                        slot_i = 0
                        dve.wait_ge(S["g0_ready"].h, 2 * (p + 1))
                        for n in range(4):
                            strm = (0, 1) if n < 2 else (0,)
                            dve.wait_ge(S["cg_done"].h, 6 * p + (2, 4, 5, 6)[n])
                            for s in strm:
                                for d in range(2):
                                    t, cb, _ = place(s, n, d)
                                    r = slice(cb, cb + 64)
                                    tt(gs[r, s, :], psw[r, 0, 256 * s:256 * s + P], g0[r, d, t, :], ALU.add, sig="cg_ready")
                            fill(slot_i)
                            fill(slot_i + 1)
                            for k, s in enumerate(strm):
                                if n == 3:
                                    break
                                dve.wait_ge(S["cn_done"].h, 5 * p + (2, 4, 5)[n])
                                dve.wait_ge(S["cn_decay"].h, 10 * p + (0, 4, 8)[n] + 2 * k + 2)
                                if s and n and p:
                                    dve.wait_ge(S["out_st"].h, 32 * p)
                                for d in range(2):
                                    _, _, c = place(s, n, d)
                                    nxt = (3 + n) if s == 0 else n + 1
                                    for hb in range(2):
                                        r = rows(hb)
                                        out = fin[r, d, :] if s and n else st[r, d, nxt, r]
                                        stt(out, psw[r, 1 + d, s * P + 64 * hb:s * P + 64 * hb + 64], pend[r, d, c:c + 1],
                                            stp[r, s, d, r], op1=ALU.add, sig="cn_ready")
                            fill(slot_i + 2)
                            slot_i += 3
                        dve.wait_ge(S["gn_done"].h, 2 * p + 1)
                        stt(yc, w(1), -1.0 / 64, yb, op1=ALU.add, sig="yc_ready")
                        dve.wait_ge(S["yroot_ready"].h, p + 1)
                        recip(yroot, yroot)
                        L.settle()
                        tt(yc, yc, yroot)
                        L.settle()
                        ts(yc, yc, par("ln_g", p), par("ln_b", p), op1=ALU.add)
                        L.settle()
                        tt(yc, yc, bonus, ALU.add)
                        L.settle()
                        tt(mixed[0][p], yc, gr, sig="o_ready")

                    dve.wait_ge(S["out_k"].h, 32 * PAIRS)
                    dve.wait_ge(S["out_st"].h, 32 * PAIRS)
                    for m in range(KT):
                        for b in range(3):
                            zi = ZM + 6 * m + 2 * b + 1
                            dve.wait_ge(z_free[(zi - 1) % 2], (zi - 1) // 2 + 1)
                            dve.wait_ge(S["z_done"].h, zi + 1)
                            tt(ctmp[2 + b] if b else merged[m], z(zi), ctmp[b], free=zi)
                            if b:
                                L.settle()
                                tt(merged[m], merged[m], ctmp[2 + b], ALU.add, sig="mrg_ready" if b == 2 else None)
                    rstd_of(1)
                    residual(0, gate1)
                    rstd_of(2)
                    normed(1)
                    for i in range(FT + 1):
                        if i < FT:
                            for v in range(2):
                                taps(ctmp[2 * (i % 2) + v], ZU + 2 * i + v, "fconv", i + FT * v)
                        if i:
                            dve.wait_ge(S["gelu_ready"].h, i)
                            c = 2 * ((i - 1) % 2)
                            tt(wact[i - 1], ctmp[c], ctmp[c + 1], sig="act_ready")
                    rstd_of(3)
                    residual(1, gate2)

                @block.gpsimd
                def _(pool):
                    L = Lane(pool, S["p_step"], z_free)
                    G = nc.gpsimd

                    def tt(out, a, b, op=ALU.mult, sig=None):
                        L.do(G.tensor_tensor(out, a, b, op), S[sig] if sig else None)

                    pool.wait_ge(S["hnorm"].h, KT)
                    L.do(G.memset(st.rearrange("p d c v -> p (d c v)"), 0.0), S["zr_ready"])
                    L.do(G.memset(s0.rearrange("p d v -> p (d v)"), 0.0), S["zr_ready"])
                    for p in range(PAIRS):
                        zb = ZP + 11 * p
                        pool.wait_ge(S["pk_in"].h, 16 * (p + 1))
                        bias = pk[:, PK["bias"]:PK["bias"] + 768].rearrange("p (n c) -> p n c", n=12)
                        tt(bias, bias, cv("colmask", 64).unsqueeze(1).to_broadcast([P, 12, 64]), ALU.add, sig="bias_ready")
                        for d in range(2):
                            pool.wait_ge(S["sig_ready"].h, 4 * p + d + 3)
                            pool.wait_ge(S["bon_done"].h, p + 1)
                            if d:
                                pool.wait_ge(S["til_ready"].h, 2 * p + 1)
                            L.do(G.tensor_scalar(kd, aa[d], par("k_a", p), omka[:, p:p + 1], ALU.mult, ALU.add), S["kd_ready"])
                            pool.wait_ge(S["scan_ready"].h, 2 * p + d + 1)
                            tt(Lx, Ls, sg[d], ALU.subtract, sig="lx_ready")
                            pool.wait_ge(S["exp_ready"].h, 6 * p + 3 * d + 2)
                            e = 0 if d else CH - 1
                            L.do(G.tensor_copy(pend[:, d, 0:2], Pc[:, e:SEQ:CH]), S["pend_ready"])
                            L.do(G.tensor_copy(pend[:, d, 2:6], Pc[:, LAT + e:TP:CH]), S["pend_ready"])
                            tt(ar[:, d, 1, :], rc, Pc, sig="rr_ready")
                        pool.wait_ge(S["til_ready"].h, 2 * (p + 1))
                        eye = ident.unsqueeze(1).to_broadcast([P, 12, P])
                        L.settle()
                        L.do(G.tensor_copy(xv, eye), S["x_init"])
                        L.do(G.tensor_copy(tvv, eye), S["x_init"])
                        for d in range(2):
                            pool.wait_ge(S["xi_ready"].h, 2 * p + d + 1)
                            pool.wait_ge(S["rope_ready"].h, 2 * (p + 1))
                            tt(qx[:, d, :], tq[:, LAT:TP], xi[:, d, :], sig="qx_ready")
            for s in handles:
                nc.gpsimd.sem_clear(s)
            nc.all_engine_barrier()

        with nc.Block() as block:
            @block.sync
            def _(sp):
                sp.dma_start(x_out, xres[:, :]).then_inc(setup, 16)
                sp.wait_ge(setup, 48 + 5 + 16)


def constants():
    import numpy as np
    c = np.zeros((P, NCN), np.float32)

    def put(name, a):
        a = np.asarray(a, np.float32).reshape(P, -1)
        c[:, CN[name]:CN[name] + a.shape[1]] = a

    i = np.arange(P)
    put("ident", np.eye(P))
    put("ones", np.ones((P, P)))
    put("blk", i[:, None] // 64 == i[None, :] // 64)
    first = i % 32 < 16
    partner = np.where(first, i + 16, i - 16)
    perm = np.zeros((P, P))
    perm[partner, i] = np.where(first, -1.0, 1.0)
    put("perm", perm)
    t = np.arange(DEC)
    inv = np.float32(10000.0) ** (-np.arange(16, dtype=np.float32) / np.float32(16))
    pos = np.where((i % 64 < 32)[:, None], t[None, :] // 64, t[None, :] % 64).astype(np.float32)
    ang = pos * inv[i % 16][:, None]
    put("cos", np.cos(ang))
    put("sin", np.sin(ang))
    reset = np.ones((2, TP))
    for s0, n in ((0, SEQ), (LAT, DEC)):
        reset[0, s0:s0 + n:CH] = 0.0
        reset[1, s0 + CH - 1:s0 + n:CH] = 0.0
    reset[:, GAP] = 0.0
    put("reset", np.broadcast_to(reset, (P, 2, TP)))
    same = i[:, None] // CH == i[None, :] // CH
    s_, t_ = i[:, None], i[None, :]
    put("tri", np.stack([same & (s_ < t_), same & (s_ <= t_), same & (s_ > t_), same & (s_ >= t_)], 1))
    lev = []
    for lv in range(LEVELS):
        b = 1 << lv
        low = (s_ // (2 * b) == t_ // (2 * b)) & (s_ % (2 * b) >= b) & (t_ % (2 * b) < b)
        lev += [low, low.T]
    put("lev", np.stack(lev, 1))
    x = np.arange(-P, DEC)[None, :] - i[:, None]
    put("posd", np.maximum(x, 0))
    put("negd", np.maximum(-x, 0))
    put("diag", x == 0)
    put("xi", np.broadcast_to(np.stack([t + 1, DEC - t]), (P, 2, DEC)))
    w, w2 = (i % 64)[:, None], np.arange(64)[None, :]
    start = np.clip(w - 8, 0, 48)
    put("colmask", np.where((w2 >= start) & (w2 < start + 16), 0.0, -1e9))
    put("zp", np.stack([SEQ - 1 - i, i], 1))
    return c


def kernel(**inputs):
    import numpy as np
    import concourse.bacc as bacc
    from concourse.bass_utils import run_bass_kernel_spmd as run

    g = {k: np.asarray(v) for k, v in inputs.items()}
    cat, f32 = np.concatenate, np.float32

    def colblocks(w):
        n = w.shape[1] // P
        return w.reshape(8, P, n, P).transpose(2, 1, 0, 3).reshape(n, P, 1024)

    def units(u):
        return u.reshape(-1, 8, P, P).transpose(0, 2, 1, 3).reshape(-1, P, 1024)

    def tiles(w):
        return w.reshape(w.shape[0] // P, P, w.shape[1] // P, P).transpose(2, 0, 1, 3)

    def channels(a):
        return a.reshape(-1, P).T

    streams, params, packs = [], [], []
    for l in range(DEPTH):
        wi = colblocks(g["w_in"][l])
        wo = units(cat([tiles(g[n][l]) for n in ("w_o_rwkv", "w_o_na", "w_o_ret")], 1).reshape(-1, P, P))
        seq = [colblocks(g["ada_w"][l]), wi[12:14]]
        for p in range(PAIRS):
            seq.append(wi[[p, 4 + p, 8 + p, 14 + p, 18 + p, 22 + p, 26 + p, 30 + p, 34 + p, 38 + p]])
        for m in range(0, 8, 2):
            a, b = [42 + 8 * i + m for i in range(3)], [43 + 8 * i + m for i in range(3)]
            j = 3 * (m // 2)
            seq += [wi[a[:1]], wo[j:j + 1], wi[a[1:]], wo[j + 1:j + 2], wi[b[:2]], wo[j + 2:j + 3], wi[b[2:]]]
        seq += [colblocks(g["w_out"][l])]
        up = colblocks(g["ffn_up"][l])
        seq += [up.reshape(2, FT, P, 1024).transpose(1, 0, 2, 3).reshape(2 * FT, P, 1024)]
        seq += [units(tiles(g["ffn_down"][l]).reshape(-1, P, P))]
        streams.append(cat(seq, 0))
        dec = g["ret_decay"][l]
        params.append(cat([
            channels(g["norm_mix_pre"][l]), channels(g["norm_mix_post"][l]), channels(g["norm_ffn_pre"][l]),
            channels(g["norm_ffn_post"][l]), channels(g["ada_b"][l]),
            g["rwkv_conv"][l].reshape(3, 14, P).transpose(2, 1, 0).reshape(P, 42),
            g["ffn_conv"][l].reshape(3, 44, P).transpose(2, 1, 0).reshape(P, 132),
            channels(g["rwkv_w0"][l]), channels(g["rwkv_a0"][l]), channels(g["rwkv_k_k"][l]),
            channels(g["rwkv_k_a"][l]), channels(g["rwkv_r_k"][l]), channels(g["rwkv_ln_g"][l]),
            channels(g["rwkv_ln_b"][l]), channels(g["ret_gn"][l]),
            channels(np.repeat(dec, 64, axis=1)), np.broadcast_to(dec.reshape(1, 16), (P, 16))], 1))
        rpb = g["na_rpb"][l][:, 4:11]
        rpb = np.pad(rpb, ((0, 0), (1, 1), (48, 49)))
        toep = np.stack([rpb[:, :, 63 - w:127 - w] for w in range(64)], 1)
        bias = cat([toep[:, :, 2:8], toep[:, :, 1:7]], 1)
        for p in range(PAIRS):
            hs, ch = slice(2 * p, 2 * p + 2), slice(p * P, (p + 1) * P)
            lora = cat([g["rwkv_w_up"][l][:, :, ch], g["rwkv_a_up"][l][:, :, ch]], 1).transpose(1, 0, 2)
            packs.append(cat([
                lora.reshape(P, 256), g["rwkv_g_up"][l][:, ch],
                g["cache_na_k"][0, l, hs].transpose(0, 2, 1).reshape(P, P),
                g["cache_na_v"][0, l, hs].transpose(1, 0, 2).reshape(P, P),
                bias[hs].transpose(1, 0, 2, 3).reshape(P, 768),
                g["state_rwkv"][0, l][:, hs].transpose(1, 3, 0, 2).reshape(P, 128),
                g["state_ret"][0, l][:, hs].transpose(1, 2, 0, 3).reshape(P, 128)], 1))

    xin = np.zeros((P, KT, TP), f32)
    xin[:, :, 0:SEQ] = g["x_prompt"][0].T.reshape(KT, P, SEQ).transpose(1, 0, 2)
    xin[:, :, LAT:] = g["x_sample"][0].T.reshape(KT, P, DEC).transpose(1, 0, 2)
    cc = np.stack([g["c_ctx"].reshape(KT, P).T, g["c"][0].reshape(KT, P).T], 2)
    ins = {
        "in_x": xin.reshape(P, -1), "in_w": np.stack(streams), "in_prm": np.stack(params),
        "in_pk": np.stack(packs).reshape(DEPTH, PAIRS, P, NPK), "in_cc": cc.reshape(P, -1), "in_const": constants(),
    }
    ins = {k: np.ascontiguousarray(v) for k, v in ins.items()}
    outs = {
        "out_x": (P, KT * TP), "out_nak": (DEPTH, PAIRS, P, SEQ), "out_nav": (DEPTH, PAIRS, SEQ, P),
        "out_srw": (DEPTH, PAIRS, P, 128), "out_srt": (DEPTH, PAIRS, P, 128),
    }
    nc = bacc.Bacc("TRN2", target_bir_lowering=False, num_devices=1)
    args = [nc.dram_tensor(k, v.shape, F32, kind="ExternalInput").ap() for k, v in ins.items()]
    args += [nc.dram_tensor(k, s, F32, kind="ExternalOutput").ap() for k, s in outs.items()]
    trunk(nc, *args)
    r = run(nc, [ins], core_ids=[0]).results[0]
    y = np.asarray(r["out_x"]).reshape(P, KT, TP).transpose(2, 1, 0).reshape(TP, D)
    k = np.asarray(r["out_nak"]).reshape(DEPTH, 8, 64, SEQ).transpose(0, 1, 3, 2)
    v = np.asarray(r["out_nav"]).reshape(DEPTH, PAIRS, SEQ, 2, 64).transpose(0, 1, 3, 2, 4).reshape(DEPTH, 8, SEQ, 64)
    rw = np.asarray(r["out_srw"]).reshape(DEPTH, PAIRS, 2, 64, 2, 64).transpose(0, 4, 1, 2, 5, 3)
    rt = np.asarray(r["out_srt"]).reshape(DEPTH, PAIRS, 2, 64, 2, 64).transpose(0, 4, 1, 2, 3, 5)
    full = np.ascontiguousarray
    return (full(y[0:SEQ][None]), full(y[LAT:][None]), full(k[None]), full(v[None]),
            full(rw.reshape(1, DEPTH, 2, 8, 64, 64)), full(rt.reshape(1, DEPTH, 2, 8, 64, 64)))
```

```python
from contextlib import ExitStack

import concourse.bass as bass
from concourse import mybir

F32 = mybir.dt.float32
F32R = mybir.dt.float32r
U32 = mybir.dt.uint32
ALU = mybir.AluOpType
ACT = mybir.ActivationFunctionType
AX = mybir.AxisListType

P = 128
D = 1024
KT = D // P
DEPTH = 2
SEQ, DEC = 128, 256
GAP = SEQ
LAT = SEQ + 2
TP = LAT + DEC
TT = [0, LAT, LAT + P]
CH = 64
PAIRS = 4
FT = 22
DECAY_C = 0.6065306597126334
RING = 5
CN_PAIR = 20
LEVELS = 6
STREAMS = [(0, 1, 0, SEQ), (1, 2, LAT, TP)]

ADA0 = 0
SHARED0 = ADA0 + 48
PAIR0 = SHARED0 + 2
MERGE0 = PAIR0 + 10 * PAIRS
OUT0 = MERGE0 + 36
UP0 = OUT0 + 8
DOWN0 = UP0 + 2 * FT
BLOCKS = DOWN0 + FT

PRM = {}
NPRM = 0
for _name, _n in (("mix_pre", 8), ("mix_post", 8), ("ffn_pre", 8), ("ffn_post", 8), ("ada_b", 48),
                  ("conv", 42), ("fconv", 132), ("w0", 8), ("a0", 8), ("k_k", 4), ("k_a", 4),
                  ("r_k", 4), ("ln_g", 4), ("ln_b", 4), ("gn", 4), ("dec_ch", 8), ("dec_hd", 16)):
    PRM[_name] = NPRM
    NPRM += _n

PK = {}
NPK = 0
for _name, _n in (("lora", 256), ("g_up", 128), ("kc", 128), ("vc", 128), ("bias", 768),
                  ("s_rw", 128), ("s_rt", 128)):
    PK[_name] = NPK
    NPK += _n

CN = {}
NCN = 0
for _name, _n in (("ident", 128), ("ones", 128), ("blk", 128), ("perm", 128), ("cos", 256), ("sin", 256),
                  ("reset", 2 * TP), ("tri", 4 * 128), ("lev", LEVELS * 2 * 128), ("posd", 384),
                  ("negd", 384), ("diag", 384), ("xi", 512), ("colmask", 64), ("zp", 2)):
    CN[_name] = NCN
    NCN += _n


class Signal:

    def __init__(self, handle):
        self.h = handle
        self.n = 0

    def by(self, ins, k=1):
        ins.then_inc(self.h, k)
        self.n += k
        return self.n


class Lane:

    def __init__(self, eng, step, z_free):
        self.eng, self.step, self.z_free = eng, step, z_free

    def do(self, ins, sig=None, free=None):
        if free is not None:
            ins.then_inc(self.z_free[free % 2], 1)
            self.last = self.z_free[free % 2], free // 2 + 1
        else:
            sig = sig or self.step
            self.last = sig.h, sig.by(ins)

    def settle(self):
        self.eng.wait_ge(*self.last)


def trunk(nc, xin, wstream, prm_d, pk_d, cc_d, const_d, x_out, nak, nav, srw, srt):
    ctx = ExitStack()
    with ctx:
        def sb(name, cols, dt=F32):
            return ctx.enter_context(nc.sbuf_tensor(name, [P, cols], dt))

        const = sb("const", NCN)
        xres = sb("xres", KT * TP)
        hbuf = sb("hbuf", KT * TP)
        mix = sb("mix", 3 * PAIRS * TP)
        ring = sb("ring", RING * 1024)
        prm = sb("prm", NPRM)
        pk = sb("pk", NPK)
        cc = sb("cc", 2 * KT)
        small = sb("small", 384)
        WORK = 6 * 1024 + 2 * (KT + FT) * TP
        work_at = nc.sbuf_base
        work = sb("work", WORK)
        part = nc.alloc_sbuf_tensor_at("part", [P, WORK], F32R, offset=work_at)
        psz = ctx.enter_context(nc.psum_tensor("psz", [P, 2, 512], F32))
        psw = ctx.enter_context(nc.psum_tensor("psw", [P, 6, 512], F32))

        def cv(name, n, a=0):
            return const[:, CN[name] + a:CN[name] + a + n]

        ident, ones, blk, perm = (cv(n, 128) for n in ("ident", "ones", "blk", "perm"))
        cosT, sinT = cv("cos", 256), cv("sin", 256)
        x = [xres[:, k * TP:(k + 1) * TP] for k in range(KT)]
        h = [hbuf[:, k * TP:(k + 1) * TP] for k in range(KT)]
        mixed = [[mix[:, (b * PAIRS + p) * TP:(b * PAIRS + p + 1) * TP] for p in range(PAIRS)] for b in range(3)]
        ring2 = [ring[:, s * 1024:(s + 1) * 1024].rearrange("p (k c) -> p k c", k=2) for s in range(RING)]
        slot = [ring[:, s * 1024:(s + 1) * 1024].rearrange("p (k c) -> p k c", k=8) for s in range(RING)]

        def par(name, i):
            return prm[:, PRM[name] + i:PRM[name] + i + 1]

        taken = [0]

        def sm(n):
            taken[0] += n
            assert taken[0] <= 384
            return small[:, taken[0] - n:taken[0]]

        mod = sm(96).rearrange("p (m s) -> p m s", s=2)
        scale1 = sm(16).rearrange("p (m s) -> p m s", s=2)
        scale2 = sm(16).rearrange("p (m s) -> p m s", s=2)
        gate1 = sm(16).rearrange("p (m s) -> p m s", s=2)
        gate2 = sm(16).rearrange("p (m s) -> p m s", s=2)
        lg = sm(24)
        lt = sm(24)
        ls = sm(24)
        lq = sm(24)
        omka = sm(4)
        eps_rms = sm(1)
        eps_rw = sm(1)
        eps_rt = sm(1)
        zeta = sm(4)
        pend = sm(12).rearrange("p (d c) -> p d c", d=2)
        mx = sm(2)
        rs = sm(2)
        ri = sm(2)
        mt = sm(2)
        cs = sm(16).rearrange("p (k s) -> p k s", s=2)

        at = [0]

        def wk(n):
            at[0] += n
            assert at[0] <= WORK, at[0]
            return work[:, at[0] - n:at[0]]

        rc, kc_, vc = (wk(TP) for _ in range(3))
        nq, nk = wk(TP), wk(TP)
        nv = wk(384).rearrange("p (t c) -> p t c", t=3)
        tq, tk = wk(TP), wk(TP)
        tv = wk(384).rearrange("p (t c) -> p t c", t=3)
        tg = wk(TP)
        kk, bonus, gr = wk(TP), wk(TP), wk(TP)
        ar = wk(4 * TP).rearrange("p (d k t) -> p d k t", d=2, k=2)
        bk = wk(4 * TP).rearrange("p (d k t) -> p d k t", d=2, k=2)
        bkt = wk(4 * 384).rearrange("p (d k t c) -> p d k t c", d=2, k=2, t=3)
        vt = wk(384).rearrange("p (t c) -> p t c", t=3)
        au = wk(12 * 512).rearrange("p (u k c) -> p u k c", u=12, k=4)
        ut = wk(6 * 128).rearrange("p (d t c) -> p d t c", d=2, t=3)
        g0 = wk(6 * 128).rearrange("p (d t c) -> p d t c", d=2, t=3)
        gs = wk(2 * 128).rearrange("p (s c) -> p s c", s=2)
        st = wk(12 * 128).rearrange("p (d c v) -> p d c v", d=2, c=6)
        stp = wk(4 * 128).rearrange("p (s d v) -> p s d v", s=2, d=2)
        fin = wk(2 * 64).rearrange("p (d v) -> p d v", d=2)
        lwal, lgl = wk(TP), wk(TP)
        dtab = wk(2 * 384).rearrange("p (h c) -> p h c", h=2)
        s0 = wk(2 * 128).rearrange("p (d v) -> p d v", d=2)
        ktz = wk(256).rearrange("p (d c) -> p d c", d=2)
        srtb = wk(2 * 64).rearrange("p (d v) -> p d v", d=2)
        inv0 = at[0]
        tvv = wk(12 * 128).rearrange("p (u c) -> p u c", u=12)
        xv = wk(12 * 128).rearrange("p (u c) -> p u c", u=12)
        gg = wk(12 * 128).rearrange("p (u c) -> p u c", u=12)
        scr = [work[:, inv0 + i * TP:inv0 + (i + 1) * TP] for i in range(11)]
        assert 11 * TP <= 36 * 128
        sg, aa = scr[0:2], scr[2:4]
        Ls, Lx, Pc, Pi, Px, kd, tb = scr[4:11]
        rest = [inv0 + 12 * 128]

        def again(n):
            rest[0] += n
            assert rest[0] <= at[0]
            return work[:, rest[0] - n:rest[0]]

        sdp = again(2 * 640).rearrange("p (h c) -> p h c", h=2)
        ropet = sdp.rearrange("p h c -> p (h c)")[:, 0:512].rearrange("p (k t) -> p k t", k=2)
        qx = again(512).rearrange("p (d t) -> p d t", d=2)
        xi = again(512).rearrange("p (d t) -> p d t", d=2)
        ysq_r = sdp.rearrange("p h c -> p (h c)")[:, 384:384 + TP]
        rroot = sdp.rearrange("p h c -> p (h c)")[:, 384 + TP:384 + 2 * TP]
        yb, yc, ysq, yroot = scr[4:8]
        scores = [again(384), sdp.rearrange("p h c -> p (h c)")[:, 0:384]]
        ptr = again(384).rearrange("p (k q) -> p k q", k=3)
        modr = work[:, 0:1536]
        whi = [part[:, i * 1024:(i + 1) * 1024] for i in range(3)]
        wlo = [part[:, (3 + i) * 1024:(4 + i) * 1024] for i in range(3)]

        def parts(first, n):
            t = [part[:, first + i * TP:first + (i + 1) * TP] for i in range(2 * n)]
            return list(zip(t[:n], t[n:]))

        hsp = parts(6 * 1024, KT)
        ybuf = [work[:, 6 * 1024 + i * TP:6 * 1024 + (i + 1) * TP] for i in range(KT)]
        o = 6 * 1024 + 2 * KT * TP
        asp = parts(o, FT)
        msp = parts(o, 3 * PAIRS)
        msp = [msp[b * PAIRS:(b + 1) * PAIRS] for b in range(3)]
        o += 6 * PAIRS * TP
        gsp = parts(o, KT)
        o += 2 * KT * TP
        rstd = work[:, o:o + TP]
        assert o + TP <= WORK
        ctmp = [mix[:, i * TP:(i + 1) * TP] for i in range(12)]
        gate = [ctmp[0:3], ctmp[3:6]]
        mprod, mraw = ctmp[6:8], ctmp[8:10]
        araw = ctmp[4:6]
        sq = ctmp[10:12]

        handles = []

        def sem(name):
            s = ctx.enter_context(nc.semaphore(name))
            handles.append(s)
            return Signal(s)

        setup = ctx.enter_context(nc.semaphore("setup"))
        w_loaded = [sem(f"w_loaded{i}") for i in range(RING)]
        
        names = """
            a_step act_hi act_lo act_raw ada_done au_done au_ready bias_ready
            bon_done bon_used bt_done bt_ready c_ready cg_done cg_ready cn_decay
            cn_done cn_ready cu_done cu_ready de_ready dt_ready exp_ready g0_done
            g0_ready g_hi g_lo gelu_ready gl_done gl_ready gn_done h_hi h_lo h_ready
            half_used hnorm kd_ready kk_ready kk_rk kk_sq kkn_done kkn_root kt_done
            kt_ready la_done lora_in lp_exp lw_done lx_ready m_hi m_lo mod_ready
            mrg_ready mx_ready no_done no_ready o_ready out_k out_st p_ready p_step
            pend_ready pk_in pn_ready prm_in pt_done pt_ready qx_ready rgn_done
            ro_ready rope_done rope_ready row_done row_ready rows_clear rr_ready
            rroot_ready rsq_ready rst_done rst_ready rt_root ry_done ry_ready
            ryc_ready s_ready sc_done scan_ready sctx_ready sd_ready sig_ready
            silu_c sq_ready sq_used ss_done st0_ready st_done til_ready tr_done
            v_step vt_done vt_ready w_hi w_lo w_used x_init x_ready x_upd xi_ready
            xt_done y_copied y_done yc_ready yroot_ready ysq_ready z_done zr_ready""".split()
        S = {n: sem(n) for n in names}
        z_free = [sem("z_free0").h, sem("z_free1").h]

        with nc.Block() as block:
            @block.sync
            def _(sp):
                sp.dma_start(const[:, :], const_d).then_inc(setup, 16)
                sp.dma_start(xres[:, :], xin).then_inc(setup, 16)
                sp.dma_start(cc[:, :], cc_d).then_inc(setup, 16)
                sp.wait_ge(setup, 48 + 5)

            @block.vector
            def _(dve):
                dve.memset(hbuf[:, :], 0.0).then_inc(setup, 1)
                dve.memset(mix[:, :], 0.0).then_inc(setup, 1)
                dve.memset(eps_rms, 1e-6).then_inc(setup, 1)
                dve.memset(eps_rw, 64e-5).then_inc(setup, 1)
                dve.memset(eps_rt, 1e-5).then_inc(setup, 1)

        with nc.Fori(0, DEPTH) as layer:
            with nc.Block() as block:
                ZPP = 13
                ZP, ZM = 2, 2 + ZPP * PAIRS
                ZO = ZM + 6 * KT
                ZU = ZO + KT
                ZD = ZU + 2 * FT

                MT = [("gate", 0, 0, 0, 0), ("gate", 0, 1, 1, 0), ("out", 0, 0, 2, 0), ("out", 0, 1, 2, 1),
                      ("gate", 0, 2, 3, 0), ("gate", 1, 0, 4, 0), ("out", 0, 2, 5, 0), ("out", 1, 0, 5, 1),
                      ("gate", 1, 1, 6, 0), ("gate", 1, 2, 7, 0), ("out", 1, 1, 8, 0), ("out", 1, 2, 8, 1)]

                def read_up(j):
                    if j < OUT0 - MERGE0:
                        last = max(i for i in range(12) if MT[i][3] == j % 9)
                        return S["z_done"].h, ZM + 12 * (j // 9) + last + 1
                    if j < DOWN0 - MERGE0:
                        return S["z_done"].h, ZO + j - (OUT0 - MERGE0) + 1
                    un = 8 * (j - (DOWN0 - MERGE0)) + 7
                    if un % FT == FT - 1:
                        return S["z_done"].h, ZD + un // FT + 1
                    return S["half_used"].h, sum(u % FT != FT - 1 for u in range(7, un + 1, 8))

                def unit(tt, d, hb):
                    return 4 * tt + 2 * d + hb

                def z(zi, n=TP):
                    return psz[:, zi % 2, 0:n]

                def w(b, a=0, n=TP):
                    return psw[:, b, a:a + n]

                def rows(hb):
                    return slice(64 * hb, 64 * hb + 64)

                def place(s, n, d):
                    if s == 0:
                        j = n if d == 0 else 3 - n
                        return 1 + j // 2, CH * (j % 2), 2 + j
                    j = n if d == 0 else 1 - n
                    return 0, CH * j, j

                def step_of(tt, half, d):
                    if tt == 0:
                        return half if d == 0 else 1 - half
                    j = 2 * (tt - 1) + half
                    return 2 + (j if d == 0 else 3 - j)

                JOBS = [(hb, kind) for hb in range(2) for kind in range(3)]

                @block.sync
                def _(sp):
                    sp.dma_start(prm[:, :], prm_d[layer]).then_inc(S["prm_in"].h, 16)
                    for b in range(RING):
                        sp.dma_start(ring[:, b * 1024:(b + 1) * 1024], wstream[layer, b]).then_inc(w_loaded[b].h, 16)
                    with sp.Fori(1, MERGE0 // RING + 1) as i:
                        for b in range(RING):
                            sp.wait_ge(S["w_used"].h, i * RING + (b - RING + 1))
                            sp.dma_start(ring[:, b * 1024:(b + 1) * 1024], wstream[layer, i * RING + b]).then_inc(w_loaded[b].h, 16)
                    with sp.Fori(MERGE0 // RING + 1, BLOCKS // RING) as i:
                        for b in range(RING):
                            sp.wait_ge(S["w_lo"].h, i * RING + (b - RING + 1 - MERGE0))
                            sp.dma_start(ring[:, b * 1024:(b + 1) * 1024], wstream[layer, i * RING + b]).then_inc(w_loaded[b].h, 16)

                @block.tensor
                def _(pe):
                    used = [0]

                    def mm(out, a, b, start=True, stop=True, sig=None):
                        ins = nc.tensor.matmul(out, a, b, start=start, stop=stop, skip_group_check=True)
                        if sig:
                            S[sig].by(ins)
                        elif used[0]:
                            S["w_used"].by(ins, used[0])
                            used[0] = 0

                    def tr(out, a, sig=None):
                        ins = nc.tensor.transpose(out, a, ident)
                        if sig:
                            S[sig].by(ins)

                    def loaded(b):
                        pe.wait_ge(w_loaded[b % RING].h, 16 * (b // RING + 1))
                        return slot[b % RING]

                    def opened(zi):
                        if zi >= 2:
                            pe.wait_ge(z_free[zi % 2], zi // 2)
                        return z(zi)

                    def dense(zi, b, src=h):
                        out, wt = opened(zi), loaded(b)
                        for k in range(KT):
                            mm(out, wt[:, k, :], src[k], k == 0, k == KT - 1, "z_done" if k == KT - 1 else None)
                        used[0] += 1

                    def turned(zi, zs, src):
                        pe.wait_ge(z_free[zs % 2], zs // 2 + 1)
                        opened(zi)
                        for t in range(3):
                            tr(psz[:, zi % 2, t * P:(t + 1) * P], src[:, TT[t]:TT[t] + P], "z_done" if t == 2 else None)

                    def sum_squares(j):
                        for k in range(KT):
                            pe.wait_ge(S["sq_ready"].h, KT * j + k + 1)
                            mm(w(0), ones, sq[k % 2], k == 0, k == KT - 1, "ss_done" if k == KT - 1 else "sq_used")

                    def mod_turned(q):
                        pe.wait_ge(S["row_ready"].h, 4 * q + 4)
                        for c in range(4):
                            tr(w(1 + q, c * P, P), modr[:, 512 * q + c * P:512 * q + c * P + P], "ada_done" if c == 3 else None)

                    sum_squares(0)
                    pe.wait_ge(S["silu_c"].h, 1)
                    for q in range(3):
                        for j in range(4):
                            for k in range(KT):
                                b = ADA0 + 4 * (4 * q + j) + k // 2
                                if k % 2 == 0:
                                    wt = loaded(b)
                                mm(psw[32 * j:32 * j + 2, 1 + q, :], cs[:, k, :], ring2[b % RING][:, k % 2, :], k == 0,
                                   k == KT - 1, "row_done" if k == KT - 1 else None)
                                used[0] += k % 2
                        for t in ((), (0,), (1, 2))[q]:
                            mod_turned(t)
                    pe.wait_ge(S["h_ready"].h, 2 * KT)
                    dense(0, SHARED0)
                    dense(1, SHARED0 + 1)

                    for p in range(PAIRS):
                        zb, bb = ZP + ZPP * p, PAIR0 + 10 * p
                        for i in range(5):
                            dense(zb + i, bb + i)
                        dense(zb + 5, bb + 5)
                        if p:
                            pe.wait_ge(S["o_ready"].h, p)
                            pe.wait_ge(S["no_ready"].h, 2 * p)
                            pe.wait_ge(S["ro_ready"].h, p)
                        pe.wait_ge(S["kk_sq"].h, p + 1)
                        mm(w(0), blk, tb, sig="kkn_done")
                        pe.wait_ge(S["kk_rk"].h, p + 1)
                        mm(w(1), blk, kd, sig="bon_done")
                        pe.wait_ge(S["pk_in"].h, 16 * (p + 1))
                        pe.wait_ge(S["lora_in"].h, 2)
                        lora = pk[:, PK["lora"]:PK["lora"] + 256]
                        for d in range(2):
                            mm(w(2 + d), lora[0:64, d * P:(d + 1) * P], lwal[0:64, :], sig="lw_done")
                        for d in range(2):
                            mm(w(4 + d), lora[64:128, d * P:(d + 1) * P], lwal[64:128, :], sig="la_done")
                        mm(opened(zb + 6), pk[:, PK["g_up"]:PK["g_up"] + P], lgl, sig="z_done")
                        dense(zb + 7, bb + 6)
                        turned(zb + 8, zb + 5, mixed[1][p])
                        dense(zb + 9, bb + 7)
                        dense(zb + 10, bb + 8)
                        dense(zb + 11, bb + 9)
                        turned(zb + 12, zb + 10, mixed[2][p])

                        pe.wait_ge(S["kkn_root"].h, p + 1)
                        for t in range(3):
                            tr(w(0, t * P, P), vc[:, TT[t]:TT[t] + P], "vt_done" if t == 2 else None)
                        pe.wait_ge(S["bon_used"].h, p + 1)
                        pe.wait_ge(S["sig_ready"].h, 4 * p + 4)
                        for d in range(2):
                            pe.wait_ge(S["til_ready"].h, 2 * p + d + 1)
                            for k in range(2):
                                for t in range(3):
                                    tr(w(1 + 2 * d + k, t * P, P), bk[:, d, k, TT[t]:TT[t] + P],
                                       "bt_done" if t == 2 else None)
                        pe.wait_ge(S["rr_ready"].h, 2 * p + 2)
                        for u in range(12):
                            t, d, hb = u // 4, u // 2 % 2, u % 2
                            b, c, r = u % 6, slice(TT[t], TT[t] + P), rows(hb)
                            if u == 0:
                                pe.wait_ge(S["vt_ready"].h, p + 1)
                            elif u < 5:
                                pe.wait_ge(S["bt_ready"].h, 4 * p + u)
                            elif u >= 6:
                                pe.wait_ge(S["au_ready"].h, 12 * p + u - 5)
                            for k in range(2):
                                mm(w(b, 256 * k, 256).rearrange("p (k c) -> p k c", k=2), bk[r, d, k, c], ar[r, d, :, c],
                                   sig="au_done" if k else None)
                        for g in range(3):
                            pe.wait_ge(S["au_ready"].h, 12 * p + max(4 * g + 4, g + 7))
                            for i in range(4):
                                tr(w(g, i * P, P), au[:, 4 * g + i, 0, :], "tr_done" if i == 3 else None)
                        for d in range(2):
                            for t in range(3):
                                for hb in range(2):
                                    mm(w(3 + d, t * P + 64 * hb, 64), au[:, unit(t, d, hb), 2, :],
                                       vt[:, t, rows(hb)], sig="g0_done" if (t, hb) == (2, 1) else None)
                        i = 0
                        for lv in range(1, LEVELS):
                            for g in range(3):
                                pe.wait_ge(S["x_ready"].h, 33 * p + 6 * (lv - 1) + 2 * g + 2)
                                for q in range(4):
                                    mm(w(g, q * P, P), au[:, 4 * g + q, 0, :], xv[:, 4 * g + q, :],
                                       sig="gl_done" if q == 3 else None)
                            for g in range(3):
                                pe.wait_ge(S["gl_ready"].h, 15 * p + 3 * (lv - 1) + g + 1)
                                for side in range(1 if lv == LEVELS - 1 else 0, 2):
                                    if i >= 3:
                                        pe.wait_ge(S["x_ready"].h, 33 * p + 6 + i - 2)
                                    elif i < 2:
                                        pe.wait_ge(S["g0_ready"].h, 2 * p + i + 1)
                                    for q in range(4):
                                        u = 4 * g + q
                                        a, b = (gg, tvv) if side else (tvv, gg)
                                        mm(w(3 + i % 3, q * P, P), a[:, u, :], b[:, u, :],
                                           sig="xt_done" if q == 3 else None)
                                    i += 1

                        pe.wait_ge(S["x_ready"].h, 33 * (p + 1))
                        pe.wait_ge(S["g0_ready"].h, 2 * p + 2)

                        def scores_mm(j):
                            hb, kind = JOBS[j]
                            q = nq[rows(hb), TT[kind]:TT[kind] + P]
                            if j == 0:
                                pe.wait_ge(S["ry_ready"].h, 2 * (p + 1))
                            else:
                                pe.wait_ge(S["s_ready"].h, 6 * p + j)
                            if kind == 0:
                                mm(w(4, 0, P), q, nk[rows(hb), 0:P], sig="sc_done")
                            else:
                                mm(w(4, 0, P), q, pk[rows(hb), PK["kc"]:PK["kc"] + P])
                                mm(w(4, P, 256), q, nk[rows(hb), LAT:TP], sig="sc_done")

                        def values_mm(j):
                            hb, kind = JOBS[j]
                            n = 3 if kind else 1
                            pe.wait_ge(S["pn_ready"].h, 6 * p + j + 1)
                            if j == 0:
                                pe.wait_ge(S["rst_ready"].h, 4 * (p + 1))
                            for i in range(n):
                                tr(w(5, i * P, P), scores[j % 2][:, i * P:(i + 1) * P], "pt_done" if i == n - 1 else None)
                            pe.wait_ge(S["pt_ready"].h, 6 * p + j + 1)
                            for i in range(n):
                                v = nv[:, i, rows(hb)]
                                if kind and i == 0:
                                    v = pk[:, PK["vc"] + 64 * hb:PK["vc"] + 64 * hb + 64]
                                mm(psw[rows(hb), 3, kind * P:(kind + 1) * P], v, ptr[:, i, :], i == 0, i == n - 1,
                                   "no_done" if i == n - 1 else None)

                        def fill(i):
                            if i == 0:
                                mm(w(4, 0, 256), perm, tq[:, LAT:TP])
                                mm(w(4, 256, 256), perm, tk[:, LAT:TP], sig="rope_done")
                                tr(w(5, 0, P), tk[:, 0:P], "kt_done")
                            elif i in (1, 2):
                                r = rows(i - 1)
                                if i == 1:
                                    pe.wait_ge(S["rope_ready"].h, 2 * (p + 1))
                                    pe.wait_ge(S["kt_ready"].h, 4 * (p + 1))
                                else:
                                    pe.wait_ge(S["sd_ready"].h, 4 * p + 2)
                                mm(w(4, 0, P), tk[r, 0:P], tq[r, 0:P])
                                mm(w(4, P, 256), tk[r, TT[1]:TT[1] + P], tq[r, LAT:TP], sig="st_done")
                                mm(w(5, 0, 256), tk[r, TT[2]:TT[2] + P], tq[r, LAT:TP], sig="st_done")
                            elif i == 3:
                                pe.wait_ge(S["sd_ready"].h, 4 * (p + 1))
                                for hb in range(2):
                                    mm(psw[rows(hb), 4, 0:P], tv[:, 0, rows(hb)], sdp[:, hb, 0:P], True, False)
                                    for t in range(2):
                                        mm(psw[rows(hb), 4, P:3 * P], tv[:, 1 + t, rows(hb)],
                                           sdp[:, hb, P + 256 * t:P + 256 * t + 256], False, False)
                                pe.wait_ge(S["qx_ready"].h, 2 * (p + 1))
                                pe.wait_ge(S["st0_ready"].h, 8 * (p + 1))
                                for d in range(2):
                                    mm(w(4, P, 256), s0[:, d, :], qx[:, d, :], False, d == 1, "ry_done" if d else None)
                                for d in range(2):
                                    mm(w(5, d * P, P), ktz[:, d, :], tv[:, 0, :], sig="rst_done" if d else None)
                            elif i < 11:
                                if i < 10:
                                    scores_mm(i - 4)
                                if i > 4:
                                    values_mm(i - 5)
                            elif i == 11:
                                pe.wait_ge(S["s_ready"].h, 6 * (p + 1))
                                mm(w(4), blk, tq, sig="rgn_done")
                                pe.wait_ge(S["rsq_ready"].h, p + 1)
                                pe.wait_ge(S["pt_ready"].h, 6 * (p + 1))
                                mm(w(5), blk, ysq_r, sig="rgn_done")

                        slot_i = 0
                        for n in range(4):
                            strm = (0, 1) if n < 2 else (0,)
                            pe.wait_ge(S["cn_ready"].h, CN_PAIR * p + (0, 8, 16, 20)[n]) if CN_PAIR * p + n else None
                            if n == 0:
                                pe.wait_ge(S["st0_ready"].h, 8 * (p + 1))
                            for s in strm:
                                for d in range(2):
                                    t, cb, _ = place(s, n, d)
                                    c = (2 + n) if s == 0 else n
                                    mm(psw[cb:cb + 64, 0, 256 * s:256 * s + P], ar[:, d, 0, TT[t] + cb:TT[t] + cb + 64],
                                       st[:, d, c, :], sig="cg_done" if d else None)
                            fill(slot_i)
                            pe.wait_ge(S["cg_ready"].h, 12 * p + (4, 8, 10, 12)[n])
                            for s in strm:
                                for d in range(2):
                                    t, cb, _ = place(s, n, d)
                                    for hb in range(2):
                                        mm(psw[cb:cb + 64, 0, 256 * s + P + 64 * hb:256 * s + P + 64 * hb + 64],
                                           tvv[cb:cb + 64, unit(t, d, hb), cb:cb + 64], gs[cb:cb + 64, s, rows(hb)],
                                           sig="cu_done" if d and hb else None)
                            fill(slot_i + 1)
                            pe.wait_ge(S["cu_ready"].h, 12 * p + (4, 8, 10, 12)[n])
                            for s in strm:
                                if n == 3:
                                    break
                                for d in range(2):
                                    t, cb, _ = place(s, n, d)
                                    o_ = psw[:, 1 + d, s * P:s * P + P]
                                    mm(o_, bkt[cb:cb + 64, d, 0, t, :], ut[cb:cb + 64, d, t, :], True, False)
                                    mm(o_, bkt[cb:cb + 64, d, 1, t, :], vt[cb:cb + 64, t, :], False, True,
                                       "cn_done" if d else None)
                            fill(slot_i + 2)
                            slot_i += 3

                        for t in range(3):
                            for d in range(2):
                                for hb in range(2):
                                    u, o_ = unit(t, d, hb), psw[rows(hb), 0, t * P:(t + 1) * P]
                                    mm(o_, vt[:, t, rows(hb)], au[:, u, 3, :], t == 0 and d == 0, False)
                                    mm(o_, ut[:, d, t, rows(hb)], au[:, u, 1, :], False, False)
                                for half in range(2):
                                    a = TT[t] + CH * half
                                    mm(w(0, t * P + CH * half, CH), st[:, d, step_of(t, half, d), :], ar[:, d, 1, a:a + CH],
                                       False, (t, d, half) == (2, 1, 1), "y_done" if (t, d, half) == (2, 1, 1) else None)
                        pe.wait_ge(S["y_copied"].h, 2 * (p + 1))
                        mm(w(1), blk, yb, sig="gn_done")
                        pe.wait_ge(S["ysq_ready"].h, p + 1)
                        mm(w(2), blk, ysq, sig="gn_done")

                    def three(out, j, c, src, first, last, sig):
                        hi, lo = src
                        a, b = whi[j % 3][:, c * P:(c + 1) * P], wlo[j % 3][:, c * P:(c + 1) * P]
                        mm(out, a, hi, first, False)
                        mm(out, a, lo, False, False)
                        mm(out, b, hi, False, last, sig)

                    def dense_split(zi, j, src, wait=None):
                        out = opened(zi)
                        pe.wait_ge(S["w_lo"].h, j + 1)
                        for k in range(KT):
                            if wait:
                                pe.wait_ge(S[wait[0]].h, wait[1] + k + 1)
                            three(out, j, k, src[k], k == 0, k == KT - 1, "z_done" if k == KT - 1 else None)

                    for mp in range(KT // 2):
                        for i, (kind, m, b, blk_, half) in enumerate(MT):
                            zi, j = ZM + 12 * mp + i, 9 * mp + blk_
                            if kind == "gate":
                                dense_split(zi, j, hsp, ("h_lo", 0) if mp == i == 0 else None)
                                continue
                            out = opened(zi)
                            pe.wait_ge(S["w_lo"].h, j + 1)
                            if mp == 0:
                                pe.wait_ge(S["m_lo"].h, PAIRS * (b + 1))
                            for k in range(PAIRS):
                                three(out, j, 4 * half + k, msp[b][k], k == 0, k == PAIRS - 1,
                                      "z_done" if k == PAIRS - 1 else None)
                    for m in range(KT):
                        dense_split(ZO + m, OUT0 - MERGE0 + m, gsp, None if m else ("g_lo", 0))
                        if m:
                            pe.wait_ge(S["sq_ready"].h, KT + m)
                            mm(w(0), ones, sq[(m - 1) % 2], m == 1, False, "sq_used")
                    pe.wait_ge(S["sq_ready"].h, 2 * KT)
                    mm(w(0), ones, sq[(KT - 1) % 2], False, True, "ss_done")
                    sum_squares(2)
                    for i in range(2 * FT):
                        dense_split(ZU + i, UP0 - MERGE0 + i, hsp, None if i else ("h_lo", KT))
                    for m in range(KT):
                        out = opened(ZD + m)
                        for k in range(FT):
                            un = FT * m + k
                            j = DOWN0 - MERGE0 + un // 8
                            if un % 8 == 0 or k == 0:
                                pe.wait_ge(S["w_lo"].h, j + 1)
                            if m == 0:
                                pe.wait_ge(S["act_lo"].h, k + 1)
                            three(out, j, un % 8, asp[k], k == 0, k == FT - 1,
                                  "z_done" if k == FT - 1 else "half_used" if un % 8 == 7 else None)
                        if m:
                            pe.wait_ge(S["sq_ready"].h, 3 * KT + m)
                            mm(w(0), ones, sq[(m - 1) % 2], m == 1, False, "sq_used")
                    pe.wait_ge(S["sq_ready"].h, 4 * KT)
                    mm(w(0), ones, sq[(KT - 1) % 2], False, True, "ss_done")

                @block.scalar
                def _(act):
                    L = Lane(act, S["a_step"], z_free)

                    def run(out, src, f=ACT.Copy, sig=None, free=None, **kw):
                        L.do(nc.scalar.activation(out, src, f, **kw), S[sig] if sig else None, free)

                    def seen(zi):
                        act.wait_ge(S["z_done"].h, zi + 1)

                    def square_out(src, k, j):
                        if k >= 2:
                            act.wait_ge(S["sq_used"].h, (KT - 1) * j + k - 1)
                        elif j:
                            act.wait_ge(S["ss_done"].h, j)
                        run(sq[k % 2], src, ACT.Square, "sq_ready")

                    def root(j):
                        act.wait_ge(S["ss_done"].h, j + 1)
                        run(rstd, w(0), ACT.Sqrt, "rt_root", scale=1.0 / D, bias=eps_rms)

                    def modulate(j, scale, shift, parts=False):
                        for k in range(KT):
                            act.wait_ge(S["hnorm"].h, KT * j + k + 1)
                            for s, _, a, b in STREAMS:
                                run(h[k][:, a:b], h[k][:, a:b], ACT.Identity, "h_ready",
                                    scale=scale[:, k, s:s + 1], bias=mod[:, shift + k, s:s + 1])
                            if parts:
                                L.settle()
                                run(hsp[k][0], h[k], sig="h_hi")

                    run(cs, cc[:, :].rearrange("p (k s) -> p k s", s=2), ACT.Silu, "silu_c")
                    for k in range(KT):
                        square_out(x[k], k, 0)
                    root(0)

                    def mod_rows(q):
                        for j in range(4):
                            act.wait_ge(S["row_done"].h, 4 * q + j + 1)
                            r = slice(32 * j, 32 * j + 2)
                            run(modr[r, 512 * q:512 * q + 512], psw[r, 1 + q, :], sig="row_ready")

                    act.wait_ge(S["prm_in"].h, 16)
                    run(lt, prm[:, PRM["dec_ch"]:PRM["dec_ch"] + 24], ACT.Abs)
                    L.settle()
                    run(lt, lt, ACT.Exp, "lp_exp", scale=-1.0)
                    act.wait_ge(S["rows_clear"].h, 1)
                    mod_rows(0)
                    mod_rows(1)
                    act.wait_ge(S["mod_ready"].h, 1)
                    modulate(0, scale1, 0)
                    mod_rows(2)

                    def centre_tap(dst, zi, name, tile):
                        seen(zi)
                        run(dst, z(zi), ACT.Identity, "c_ready", scale=par(name, 3 * tile + 1), bias=0.0)

                    centre_tap(lwal, 0, "conv", 12)
                    centre_tap(lgl, 1, "conv", 13)
                    act.wait_ge(z_free[0], 1)
                    run(lwal[0:64, :], lwal[0:64, :], ACT.Tanh, "lora_in")
                    act.wait_ge(z_free[1], 1)
                    run(lgl, lgl, ACT.Sigmoid, "lora_in")

                    def load_pack(p):
                        act.dma_start(pk[:, :], pk_d[layer, p]).then_inc(S["pk_in"].h, 16)

                    load_pack(0)
                    for p in range(PAIRS):
                        zb = ZP + ZPP * p
                        if p:
                            act.wait_ge(S["til_ready"].h, 2 * p)
                            act.wait_ge(S["rr_ready"].h, 2 * p)
                        for i, dst in enumerate((rc, kc_, vc)):
                            centre_tap(dst, zb + i, "conv", 4 * i + p)
                        seen(zb + 3)
                        run(nq, z(zb + 3), free=zb + 3, scale=0.125)
                        seen(zb + 4)
                        if p:
                            act.wait_ge(S["out_k"].h, 32 * p)
                        run(nk, z(zb + 4), free=zb + 4)
                        L.settle()
                        act.dma_start(nak[layer, p], nk[:, 0:P]).then_inc(S["out_k"].h, 16)
                        seen(zb + 5)
                        run(mixed[1][p], z(zb + 5), free=zb + 5)
                        if p:
                            act.wait_ge(S["o_ready"].h, p)
                            act.wait_ge(S["ro_ready"].h, p)
                        act.wait_ge(S["kkn_done"].h, p + 1)
                        run(Pi, w(0), ACT.Sqrt, "kkn_root")
                        for d in range(2):
                            act.wait_ge(S["lw_done"].h, 2 * p + d + 1)
                            run(sg[d], w(2 + d), ACT.Sigmoid, "sig_ready", bias=par("w0", 4 * d + p))
                        for d in range(2):
                            act.wait_ge(S["la_done"].h, 2 * p + d + 1)
                            run(aa[d], w(4 + d), ACT.Sigmoid, "sig_ready", bias=par("a0", 4 * d + p))
                        seen(zb + 6)
                        run(gr, z(zb + 6), free=zb + 6)
                        seen(zb + 7)
                        run(tq, z(zb + 7), free=zb + 7)
                        seen(zb + 8)
                        run(nv, z(zb + 8, 384).rearrange("p (t c) -> p t c", t=3), free=zb + 8)
                        L.settle()
                        act.dma_start(nav[layer, p], nv[:, 0, :]).then_inc(S["out_k"].h, 16)
                        seen(zb + 9)
                        run(tk, z(zb + 9), free=zb + 9, scale=0.125)
                        act.wait_ge(S["kk_ready"].h, p + 1)
                        for d in range(2):
                            if d:
                                act.wait_ge(S["til_ready"].h, 2 * p + 1)
                                act.wait_ge(S["rr_ready"].h, 2 * p + 1)
                            act.wait_ge(S["scan_ready"].h, 2 * p + d + 1)
                            run(Pi, Ls, ACT.Exp, "exp_ready", scale=DECAY_C)
                            run(Pc, Ls, ACT.Exp, "exp_ready", scale=-DECAY_C)
                            act.wait_ge(S["lx_ready"].h, 2 * p + d + 1)
                            run(Px, Lx, ACT.Exp, "exp_ready", scale=-DECAY_C)
                            if d == 0:
                                seen(zb + 10)
                                run(mixed[2][p], z(zb + 10), free=zb + 10)
                                seen(zb + 11)
                                run(tg, z(zb + 11), ACT.Silu, free=zb + 11)
                                seen(zb + 12)
                                run(tv, z(zb + 12, 384).rearrange("p (t c) -> p t c", t=3), free=zb + 12)
                        act.wait_ge(S["vt_done"].h, p + 1)
                        run(vt, w(0, 0, 384).rearrange("p (t c) -> p t c", t=3), sig="vt_ready")
                        for d in range(2):
                            for k in range(2):
                                act.wait_ge(S["bt_done"].h, 4 * p + 2 * d + k + 1)
                                run(bkt[:, d, k], w(1 + 2 * d + k, 0, 384).rearrange("p (t c) -> p t c", t=3), sig="bt_ready")
                        for d in range(2):
                            for hb in range(2):
                                r = rows(hb)
                                run(st[r, d, 2, r], pk[r, PK["s_rw"] + 64 * d:PK["s_rw"] + 64 * d + 64], sig="st0_ready")
                                run(s0[r, d, r], pk[r, PK["s_rt"] + 64 * d:PK["s_rt"] + 64 * d + 64], sig="st0_ready")
                        for d in range(2):
                            act.wait_ge(S["g0_done"].h, 2 * p + d + 1)
                            run(g0[:, d], w(3 + d, 0, 384).rearrange("p (t c) -> p t c", t=3), sig="g0_ready")
                        for lv in range(1, LEVELS):
                            for g in range(3):
                                act.wait_ge(S["gl_done"].h, 15 * p + 3 * (lv - 1) + g + 1)
                                run(gg[:, 4 * g:4 * g + 4, :], w(g, 0, 512).rearrange("p (u c) -> p u c", u=4), sig="gl_ready")
                            if lv == 1:
                                for hb in range(2):
                                    act.wait_ge(S["dt_ready"].h, 2 * p + hb + 1)
                                    run(dtab[:, hb, :], dtab[:, hb, :], ACT.Exp, "de_ready")
                                for d in range(2):
                                    for hb in range(2):
                                        i = 8 + 8 * d + 2 * p + hb
                                        run(zeta[:, 2 * d + hb:2 * d + hb + 1], cv("zp", 1, d), ACT.Exp,
                                            scale=lg[:, i:i + 1])
                        act.wait_ge(S["xt_done"].h, 27 * (p + 1))

                        def scores_act(j):
                            hb, kind = JOBS[j]
                            act.wait_ge(S["sc_done"].h, 6 * p + j + 1)
                            if j >= 2:
                                act.wait_ge(S["pt_done"].h, 6 * p + j - 1)
                            run(scores[j % 2][:, 0:P], w(4, 0, P), sig="sctx_ready")

                        def probs_t(j):
                            n = 3 if JOBS[j][1] else 1
                            act.wait_ge(S["pt_done"].h, 6 * p + j + 1)
                            if j:
                                act.wait_ge(S["no_done"].h, 6 * p + j)
                            run(ptr[:, 0:n, :], w(5, 0, n * P).rearrange("p (k q) -> p k q", k=n), sig="pt_ready")

                        def exps(j):
                            n = 384 if JOBS[j][1] else P
                            act.wait_ge(S["mx_ready"].h, 6 * p + j + 1)
                            s_ = scores[j % 2][:, 0:n]
                            run(s_, s_, ACT.Exp, "p_ready", bias=mx[:, j % 2:j % 2 + 1], accum_out=rs[:, j % 2:j % 2 + 1])

                        def fill(i):
                            if i == 0:
                                for d in range(2):
                                    if d == 0:
                                        act.wait_ge(S["kt_done"].h, p + 1)
                                        L.settle()
                                    for hb in range(2):
                                        run(ktz[:, d, rows(hb)], w(5, 64 * hb, 64), ACT.Copy, "kt_ready",
                                            scale=zeta[:, 2 * d + hb:2 * d + hb + 1])
                                for d in range(2):
                                    run(xi[:, d, :], cv("xi", 256, 256 * d), ACT.Exp, "xi_ready",
                                        scale=lg[:, 4 * d + p:4 * d + p + 1])
                            elif i == 3:
                                act.wait_ge(S["ry_done"].h, p + 1)
                                run(tq[:, 0:P], w(4, 0, P), sig="ry_ready")
                                run(tq[:, LAT:TP], w(4, P, 256), sig="ry_ready")
                                act.wait_ge(S["rst_done"].h, p + 1)
                                if p:
                                    act.wait_ge(S["out_st"].h, 32 * p)
                                for d in range(2):
                                    for hb in range(2):
                                        run(srtb[rows(hb), d, :], psw[rows(hb), 5, d * P + 64 * hb:d * P + 64 * hb + 64],
                                            sig="rst_ready")
                                L.settle()
                                act.dma_start(srt[layer, p], srtb.rearrange("p d v -> p (d v)")).then_inc(S["out_st"].h, 16)
                            elif 4 <= i < 11:
                                if i < 10:
                                    scores_act(i - 4)
                                if i > 4:
                                    probs_t(i - 5)
                                if i < 10:
                                    exps(i - 4)
                            elif i == 11:
                                act.wait_ge(S["no_done"].h, 6 * (p + 1))
                                run(mixed[1][p][:, 0:P], w(3, 0, P), sig="no_ready")
                                run(mixed[1][p][:, LAT:TP], w(3, P, 256), sig="no_ready")
                                act.wait_ge(S["ryc_ready"].h, p + 1)
                                run(ysq_r, tk, ACT.Square, "rsq_ready")
                                act.wait_ge(S["rgn_done"].h, 2 * (p + 1))
                                run(rroot, w(5), ACT.Sqrt, "rroot_ready", scale=1.0 / 64, bias=eps_rt)

                        slot_i = 0
                        for n in range(4):
                            strm = (0, 1) if n < 2 else (0,)
                            if n == 0:
                                act.wait_ge(S["pend_ready"].h, 4 * (p + 1))
                                L.settle()
                            for k, s in enumerate(strm):
                                if n == 3:
                                    break
                                if n:
                                    act.wait_ge(S["cn_ready"].h, CN_PAIR * p + (0, 4, 12, 20)[n] + 4 * k)
                                for d in range(2):
                                    _, _, c = place(s, n, d)
                                    run(stp[:, s, d, :], st[:, d, (2 + n) if s == 0 else n, :], ACT.Copy, "cn_decay",
                                        scale=pend[:, d, c:c + 1])
                            fill(slot_i)
                            act.wait_ge(S["cu_done"].h, 6 * p + (2, 4, 5, 6)[n])
                            for s in strm:
                                for d in range(2):
                                    t, cb, _ = place(s, n, d)
                                    run(ut[cb:cb + 64, d, t, :], psw[cb:cb + 64, 0, 256 * s + P:256 * s + 2 * P], sig="cu_ready")
                            fill(slot_i + 1)
                            fill(slot_i + 2)
                            slot_i += 3
                        act.wait_ge(S["cn_ready"].h, CN_PAIR * p + 16)
                        act.dma_start(srw[layer, p], fin.rearrange("p d v -> p (d v)")).then_inc(S["out_st"].h, 16)
                        act.wait_ge(S["y_done"].h, p + 1)
                        run(yb[:, 0:P], w(0, 0, P), sig="y_copied")
                        run(yb[:, LAT:TP], w(0, P, 256), sig="y_copied")
                        act.wait_ge(S["yc_ready"].h, p + 1)
                        run(ysq, yc, ACT.Square, "ysq_ready")
                        act.wait_ge(S["gn_done"].h, 2 * (p + 1))
                        run(yroot, w(2), ACT.Sqrt, "yroot_ready", scale=1.0 / 64, bias=eps_rw)
                        if p + 1 < PAIRS:
                            act.wait_ge(S["s_ready"].h, 6 * (p + 1))
                            load_pack(p + 1)

                    def split(j):
                        if j >= BLOCKS - MERGE0:
                            return
                        b = MERGE0 + j
                        act.wait_ge(w_loaded[b % RING].h, 16 * (b // RING + 1))
                        if j >= 3:
                            act.wait_ge(*read_up(j - 3))
                        run(whi[j % 3], ring[:, b % RING * 1024:(b % RING + 1) * 1024], sig="w_hi")

                    act.wait_ge(S["o_ready"].h, PAIRS)
                    act.wait_ge(S["ro_ready"].h, PAIRS)
                    act.wait_ge(S["out_k"].h, 32 * PAIRS)
                    act.wait_ge(S["out_st"].h, 32 * PAIRS)
                    split(0)
                    for k in range(KT):
                        run(hsp[k][0], h[k], sig="h_hi")
                    split(1)
                    split(2)
                    for b in range(3):
                        for k in range(PAIRS):
                            run(msp[b][k][0], mixed[b][k], sig="m_hi")

                    def merged_hi(m):
                        act.wait_ge(S["mrg_ready"].h, m + 1)
                        run(gsp[m][0], mraw[m % 2], sig="g_hi")

                    act.wait_ge(S["m_lo"].h, 3 * PAIRS)
                    for mp in range(KT // 2):
                        for i, (kind, m, b, blk_, half) in enumerate(MT):
                            zi, mm_ = ZM + 12 * mp + i, 2 * mp + m
                            if kind == "gate":
                                seen(zi)
                                if mm_ >= 2:
                                    act.wait_ge(S["mrg_ready"].h, mm_ - 1)
                                run(gate[m][b], z(zi), ACT.Sigmoid, free=zi)
                            if i == 11 or MT[i + 1][3] != blk_:
                                split(9 * mp + blk_ + 3)
                            if i == 8:
                                merged_hi(2 * mp)
                            if i == 0 and mp:
                                merged_hi(2 * mp - 1)
                    merged_hi(KT - 1)
                    for m in range(KT):
                        seen(ZO + m)
                        square_out(z(ZO + m), m, 1)
                        run(ybuf[m], z(ZO + m), free=ZO + m)
                        split(OUT0 - MERGE0 + m + 3)
                    root(1)
                    for k in range(KT):
                        act.wait_ge(S["x_upd"].h, k + 1)
                        square_out(x[k], k, 2)
                    root(2)
                    modulate(1, scale2, 24, True)

                    for i in range(FT + 2):
                        if i < FT:
                            if i >= 2:
                                act.wait_ge(S["act_raw"].h, i - 1)
                            for v in range(2):
                                centre_tap(ctmp[2 * (i % 2) + v], ZU + 2 * i + v, "fconv", i + FT * v)
                                split(UP0 - MERGE0 + 2 * i + v + 3)
                        if 1 <= i <= FT:
                            zi = ZU + 2 * i - 1
                            act.wait_ge(z_free[zi % 2], zi // 2 + 1)
                            g_ = ctmp[2 * ((i - 1) % 2) + 1]
                            run(g_, g_, ACT.Gelu_apprx_tanh, "gelu_ready")
                        if i >= 2:
                            act.wait_ge(S["act_raw"].h, i - 1)
                            run(asp[i - 2][0], araw[i % 2], sig="act_hi")
                    d0 = DOWN0 - MERGE0
                    for m in range(KT):
                        for un in range(FT * m, FT * m + FT):
                            if un % 8 == 7 and un % FT != FT - 1:
                                split(d0 + un // 8 + 3)
                        seen(ZD + m)
                        square_out(z(ZD + m), m, 3)
                        run(ybuf[m], z(ZD + m), free=ZD + m)
                        if (FT * m + FT) % 8 == 0:
                            split(d0 + FT * (m + 1) // 8 - 1 + 3)
                    root(3)

                @block.vector
                def _(dve):
                    L = Lane(dve, S["v_step"], z_free)
                    V = nc.vector

                    def sig_of(sig, free):
                        return S[sig] if sig else None, free

                    def tt(out, a, b, op=ALU.mult, sig=None, free=None):
                        L.do(V.tensor_tensor(out, a, b, op), *sig_of(sig, free))

                    def ts(out, a, s1, s2=None, op0=ALU.mult, op1=ALU.bypass, sig=None):
                        L.do(V.tensor_scalar(out, a, s1, s2, op0, op1), *sig_of(sig, None))

                    def stt(out, a, s_, b, op0=ALU.mult, op1=ALU.mult, sig=None, free=None):
                        L.do(V.scalar_tensor_tensor(out, a, s_, b, op0, op1), *sig_of(sig, free))

                    def recip(out, a, sig=None):
                        L.do(V.reciprocal(out, a), *sig_of(sig, None))

                    def pred(out, mask, data, sig):
                        L.do(V.copy_predicated(out, mask, data), S[sig])

                    def normed(j):
                        for k in range(KT):
                            for s, _, a, b in STREAMS:
                                tt(h[k][:, a:b], x[k][:, a:b], rstd[:, a:b], sig="hnorm" if s else None)

                    def rstd_of(j):
                        dve.wait_ge(S["rt_root"].h, j + 1)
                        recip(rstd, rstd)
                        L.settle()

                    def residual(j, gate):
                        for k in range(KT):
                            tt(ybuf[k], ybuf[k], rstd)
                            L.settle()
                            for s, _, a, b in STREAMS:
                                stt(x[k][:, a:b], ybuf[k][:, a:b], gate[:, k, s:s + 1], x[k][:, a:b], op1=ALU.add,
                                    sig="x_upd" if s else None)

                    def taps(dst, zi, name, tile):
                        taps.n += 1
                        dve.wait_ge(S["c_ready"].h, taps.n)
                        zt = z(zi)
                        stt(dst[:, 1:TP], zt[:, 0:TP - 1], par(name, 3 * tile), dst[:, 1:TP], op1=ALU.add)
                        L.settle()
                        stt(dst[:, 0:TP - 1], zt[:, 1:TP], par(name, 3 * tile + 2), dst[:, 0:TP - 1], op1=ALU.add, free=zi)

                    taps.n = 0

                    dve.wait_ge(S["prm_in"].h, 16)
                    dec = prm[:, PRM["dec_ch"]:PRM["dec_ch"] + 24]
                    ts(omka, prm[:, PRM["k_a"]:PRM["k_a"] + 4], -1.0, 1.0, op1=ALU.add)
                    ts(lg, dec, 0.0, op0=ALU.min)
                    dve.wait_ge(S["lp_exp"].h, 1)
                    ts(ls, lt, 2.0, op0=ALU.add)
                    L.settle()
                    recip(ls, ls)
                    L.settle()
                    tt(ls, ls, lt)
                    L.settle()
                    tt(lt, ls, ls)
                    L.settle()
                    ts(lq, lt, 1.0 / 17)
                    for i in range(7, 0, -1):
                        L.settle()
                        stt(lq, lq, 1.0 / (2 * i + 1), lt, op0=ALU.add)
                    L.settle()
                    stt(lq, lq, 1.0, ls, op0=ALU.add)
                    L.settle()
                    stt(lg, lq, -2.0, lg, op1=ALU.add)
                    rstd_of(0)
                    normed(0)
                    def both(name):
                        return prm[:, PRM[name]:PRM[name] + KT].unsqueeze(2).to_broadcast([P, KT, 2])

                    def mod_of(q):
                        dve.wait_ge(S["ada_done"].h, q + 1)
                        for j in range(4):
                            m = 16 * q + 4 * j
                            tt(mod[:, m:m + 4], psw[:, 1 + q, :].rearrange("p (c r) -> p c r", c=4)[:, :, 32 * j:32 * j + 2],
                               prm[:, PRM["ada_b"] + m:PRM["ada_b"] + m + 4].unsqueeze(2).to_broadcast([P, 4, 2]), ALU.add)
                        L.settle()

                    mod_of(0)
                    stt(scale1, mod[:, 8:16], 1.0, both("mix_pre"), op0=ALU.add, sig="mod_ready")
                    mod_of(1)
                    tt(gate1, mod[:, 16:24], both("mix_post"))
                    mod_of(2)
                    stt(scale2, mod[:, 32:40], 1.0, both("ffn_pre"), op0=ALU.add)
                    tt(gate2, mod[:, 40:48], both("ffn_post"))
                    taps(lwal, 0, "conv", 12)
                    taps(lgl, 1, "conv", 13)

                    def level_masks(lv):
                        m = cv("lev", 256, 256 * lv).bitcast(U32).rearrange("p (d c) -> p d c", d=2)
                        m0 = m.unsqueeze(2).to_broadcast([P, 2, 2, P])
                        m1 = m[:, ::-1, :].unsqueeze(2).to_broadcast([P, 2, 2, P])
                        return m0, m1

                    def four(a):
                        return a.rearrange("p (d q) c -> p d q c", d=2)

                    for p in range(PAIRS):
                        zb = ZP + ZPP * p
                        for i, dst in enumerate((rc, kc_, vc)):
                            taps(dst, zb + i, "conv", 4 * i + p)
                        L.settle()
                        ts(kk, kc_, par("k_k", p))
                        stt(kd, rc, par("r_k", p), kc_, sig="kk_rk")
                        L.settle()
                        tt(tb, kk, kk, sig="kk_sq")
                        dve.wait_ge(S["bon_done"].h, p + 1)
                        tt(bonus, w(1), vc, sig="bon_used")
                        dve.wait_ge(S["kkn_root"].h, p + 1)
                        ts(Pi, Pi, 1e-12, op0=ALU.max)
                        L.settle()
                        recip(Pi, Pi)
                        L.settle()
                        tt(kk, kk, Pi, sig="kk_ready")
                        for d in range(2):
                            L.settle()
                            dve.wait_ge(S["sig_ready"].h, 4 * p + d + 1)
                            rst = cv("reset", TP, TP * d)
                            order = slice(None, None, -1) if d else slice(None)
                            L.do(V.tensor_tensor_scan(Ls[:, order], rst[:, order], sg[d][:, order], 0.0, ALU.mult, ALU.add),
                                 S["scan_ready"])
                            dve.wait_ge(S["sig_ready"].h, 4 * p + d + 3)
                            L.settle()
                            tt(tb, kk, aa[d])
                            dve.wait_ge(S["kd_ready"].h, 2 * p + d + 1)
                            tt(kd, kd, kc_)
                            L.settle()
                            dve.wait_ge(S["exp_ready"].h, 6 * p + 3 * d + 3)
                            stt(ar[:, d, 0, :], kk, -1.0, Px)
                            tt(bk[:, d, 1, :], kd, Pi)
                            tt(bk[:, d, 0, :], tb, Pi, sig="til_ready")
                        for u in range(12):
                            d = u // 2 % 2
                            dve.wait_ge(S["au_done"].h, 12 * p + u + 1)
                            tt(au[:, u].rearrange("p (k e) c -> p k (e c)", k=2),
                               w(u % 6, 0, 512).rearrange("p (k c) -> p k c", k=2),
                               cv("tri", 256, 256 * d).unsqueeze(1).to_broadcast([P, 2, 256]), sig="au_ready")
                        dve.wait_ge(S["x_init"].h, 2 * (p + 1))
                        m0, m1 = level_masks(0)
                        for g in range(3):
                            dve.wait_ge(S["tr_done"].h, 3 * p + g + 1)
                            us = slice(4 * g, 4 * g + 4)
                            pred(four(xv[:, us]), m0, w(g, 0, 512).rearrange("p (d q c) -> p d q c", d=2, q=2), "x_ready")
                            pred(four(tvv[:, us]), m1, four(au[:, us, 0, :]), "x_ready")
                        for hb in range(2):
                            i = 8 + 2 * p + hb
                            ts(dtab[:, hb, :], cv("posd", 384), lg[:, i:i + 1])
                            L.settle()
                            stt(dtab[:, hb, :], cv("negd", 384), lg[:, i + 8:i + 9], dtab[:, hb, :], op1=ALU.add, sig="dt_ready")
                        i = 0
                        for lv in range(1, LEVELS):
                            m0, m1 = level_masks(lv)
                            for g in range(3):
                                us = slice(4 * g, 4 * g + 4)
                                for side in range(1 if lv == LEVELS - 1 else 0, 2):
                                    dve.wait_ge(S["xt_done"].h, 27 * p + i + 1)
                                    pred(four((tvv if side else xv)[:, us]), m1 if side else m0,
                                         w(3 + i % 3, 0, 512).rearrange("p (d q c) -> p d q c", d=2, q=2), "x_ready")
                                    i += 1

                        def softmax(j):
                            hb, kind = JOBS[j]
                            s_ = scores[j % 2]
                            dve.wait_ge(S["sctx_ready"].h, 6 * p + j + 1)
                            if kind:
                                a = PK["bias"] + 384 * hb + (P if kind == 1 else 0)
                                if j == 1:
                                    dve.wait_ge(S["bias_ready"].h, p + 1)
                                tt(s_[:, P:384], w(4, P, 256), pk[:, a:a + 256], ALU.add)
                                L.settle()
                            n = 384 if kind else P
                            L.do(V.tensor_reduce(mt[:, 0:1], s_[:, 0:n], AX.X, ALU.max), S["s_ready"])
                            L.settle()
                            ts(mx[:, j % 2:j % 2 + 1], mt[:, 0:1], -1.0, sig="mx_ready")
                            dve.wait_ge(S["p_ready"].h, 6 * p + j + 1)
                            recip(ri[:, j % 2:j % 2 + 1], rs[:, j % 2:j % 2 + 1])
                            L.settle()
                            ts(s_[:, 0:n], s_[:, 0:n], ri[:, j % 2:j % 2 + 1], sig="pn_ready")

                        def fill(i):
                            if i == 0:
                                dve.wait_ge(S["de_ready"].h, 2 * (p + 1))
                                tt(dtab, dtab, cv("diag", 384).unsqueeze(1).to_broadcast([P, 2, 384]), ALU.add)
                                dve.wait_ge(S["rope_done"].h, p + 1)
                                tt(ropet, w(4, 0, 512).rearrange("p (k t) -> p k t", k=2),
                                   sinT.unsqueeze(1).to_broadcast([P, 2, 256]))
                                tt(tq[:, LAT:TP], tq[:, LAT:TP], cosT)
                                tt(tk[:, LAT:TP], tk[:, LAT:TP], cosT)
                                L.settle()
                                tt(tq[:, LAT:TP], tq[:, LAT:TP], ropet[:, 0], ALU.add, sig="rope_ready")
                                tt(tk[:, LAT:TP], tk[:, LAT:TP], ropet[:, 1], ALU.add, sig="rope_ready")
                            elif i in (1, 2):
                                hb = i - 1
                                dve.wait_ge(S["st_done"].h, 4 * p + 2 * hb + 1)
                                tt(sdp[:, hb, 0:P], w(4, 0, P), dtab[:, hb, P:2 * P])
                                tt(sdp[:, hb, P:384], w(4, P, 256), dtab[:, hb, P:384], sig="sd_ready")
                                dve.wait_ge(S["st_done"].h, 4 * p + 2 * hb + 2)
                                tt(sdp[:, hb, 384:640], w(5, 0, 256), dtab[:, hb, 0:256], sig="sd_ready")
                            elif 4 <= i < 10:
                                softmax(i - 4)
                            elif i == 11:
                                dve.wait_ge(S["rgn_done"].h, 2 * p + 1)
                                stt(tk, w(4), -1.0 / 64, tq, op1=ALU.add, sig="ryc_ready")
                                dve.wait_ge(S["rroot_ready"].h, p + 1)
                                recip(rroot, rroot)
                                L.settle()
                                tt(tk, tk, rroot)
                                L.settle()
                                stt(mixed[2][p], tk, par("gn", p), tg, sig="ro_ready")

                        slot_i = 0
                        dve.wait_ge(S["g0_ready"].h, 2 * (p + 1))
                        for n in range(4):
                            strm = (0, 1) if n < 2 else (0,)
                            dve.wait_ge(S["cg_done"].h, 6 * p + (2, 4, 5, 6)[n])
                            for s in strm:
                                for d in range(2):
                                    t, cb, _ = place(s, n, d)
                                    r = slice(cb, cb + 64)
                                    tt(gs[r, s, :], psw[r, 0, 256 * s:256 * s + P], g0[r, d, t, :], ALU.add, sig="cg_ready")
                            fill(slot_i)
                            fill(slot_i + 1)
                            for k, s in enumerate(strm):
                                if n == 3:
                                    break
                                dve.wait_ge(S["cn_done"].h, 5 * p + (2, 4, 5)[n])
                                dve.wait_ge(S["cn_decay"].h, 10 * p + (0, 4, 8)[n] + 2 * k + 2)
                                if s and n and p:
                                    dve.wait_ge(S["out_st"].h, 32 * p)
                                for d in range(2):
                                    _, _, c = place(s, n, d)
                                    nxt = (3 + n) if s == 0 else n + 1
                                    for hb in range(2):
                                        r = rows(hb)
                                        out = fin[r, d, :] if s and n else st[r, d, nxt, r]
                                        stt(out, psw[r, 1 + d, s * P + 64 * hb:s * P + 64 * hb + 64], pend[r, d, c:c + 1],
                                            stp[r, s, d, r], op1=ALU.add, sig="cn_ready")
                            fill(slot_i + 2)
                            slot_i += 3
                        dve.wait_ge(S["gn_done"].h, 2 * p + 1)
                        stt(yc, w(1), -1.0 / 64, yb, op1=ALU.add, sig="yc_ready")
                        dve.wait_ge(S["yroot_ready"].h, p + 1)
                        recip(yroot, yroot)
                        L.settle()
                        tt(yc, yc, yroot)
                        L.settle()
                        ts(yc, yc, par("ln_g", p), par("ln_b", p), op1=ALU.add)
                        L.settle()
                        tt(yc, yc, bonus, ALU.add)
                        L.settle()
                        tt(mixed[0][p], yc, gr, sig="o_ready")

                    def lo_of(parts, raw, sig, hi_sig, n):
                        dve.wait_ge(S[hi_sig].h, n)
                        tt(parts[1], raw, parts[0].bitcast(F32), ALU.subtract, sig=sig)

                    for k in range(KT):
                        lo_of(hsp[k], h[k], "h_lo", "h_hi", k + 1)
                    for b in range(3):
                        for k in range(PAIRS):
                            lo_of(msp[b][k], mixed[b][k], "m_lo", "m_hi", PAIRS * b + k + 1)

                    zg = {}
                    L.settle()
                    for mp in range(KT // 2):
                        for i, (kind, m, b, blk_, half) in enumerate(MT):
                            zi, mm_ = ZM + 12 * mp + i, 2 * mp + m
                            if kind == "gate":
                                zg[m, b] = zi
                                continue
                            dve.wait_ge(z_free[zg[m, b] % 2], zg[m, b] // 2 + 1)
                            dve.wait_ge(S["z_done"].h, zi + 1)
                            if b == 0:
                                tt(mraw[m], z(zi), gate[m][0], free=zi)
                                if mm_:
                                    lo_of(gsp[mm_ - 1], mraw[1 - m], "g_lo", "g_hi", mm_)
                                continue
                            tt(mprod[b - 1], z(zi), gate[m][b], free=zi)
                            L.settle()
                            tt(mraw[m], mraw[m], mprod[b - 1], ALU.add, sig="mrg_ready" if b == 2 else None)
                    lo_of(gsp[KT - 1], mraw[1], "g_lo", "g_hi", KT)
                    rstd_of(1)
                    residual(0, gate1)
                    rstd_of(2)
                    normed(1)
                    for k in range(KT):
                        lo_of(hsp[k], h[k], "h_lo", "h_hi", KT + k + 1)
                    for i in range(FT + 2):
                        if i < FT:
                            for v in range(2):
                                taps(ctmp[2 * (i % 2) + v], ZU + 2 * i + v, "fconv", i + FT * v)
                        if i >= 2:
                            lo_of(asp[i - 2], araw[i % 2], "act_lo", "act_hi", i - 1)
                            L.settle()
                        if 1 <= i <= FT:
                            dve.wait_ge(S["gelu_ready"].h, i)
                            c = 2 * ((i - 1) % 2)
                            tt(araw[(i - 1) % 2], ctmp[c], ctmp[c + 1], sig="act_raw")
                    rstd_of(3)
                    residual(1, gate2)

                @block.gpsimd
                def _(pool):
                    L = Lane(pool, S["p_step"], z_free)
                    G = nc.gpsimd

                    def tt(out, a, b, op=ALU.mult, sig=None):
                        L.do(G.tensor_tensor(out, a, b, op), S[sig] if sig else None)

                    L.do(G.memset(modr, 0.0), S["rows_clear"])
                    pool.wait_ge(S["hnorm"].h, KT)
                    L.do(G.memset(st.rearrange("p d c v -> p (d c v)"), 0.0), S["zr_ready"])
                    L.do(G.memset(s0.rearrange("p d v -> p (d v)"), 0.0), S["zr_ready"])
                    for p in range(PAIRS):
                        zb = ZP + ZPP * p
                        pool.wait_ge(S["pk_in"].h, 16 * (p + 1))
                        bias = pk[:, PK["bias"]:PK["bias"] + 768].rearrange("p (n c) -> p n c", n=12)
                        tt(bias, bias, cv("colmask", 64).unsqueeze(1).to_broadcast([P, 12, 64]), ALU.add, sig="bias_ready")
                        for d in range(2):
                            pool.wait_ge(S["sig_ready"].h, 4 * p + d + 3)
                            pool.wait_ge(S["bon_done"].h, p + 1)
                            if d:
                                pool.wait_ge(S["til_ready"].h, 2 * p + 1)
                            L.do(G.tensor_scalar(kd, aa[d], par("k_a", p), omka[:, p:p + 1], ALU.mult, ALU.add), S["kd_ready"])
                            pool.wait_ge(S["scan_ready"].h, 2 * p + d + 1)
                            tt(Lx, Ls, sg[d], ALU.subtract, sig="lx_ready")
                            pool.wait_ge(S["exp_ready"].h, 6 * p + 3 * d + 2)
                            e = 0 if d else CH - 1
                            L.do(G.tensor_copy(pend[:, d, 0:2], Pc[:, e:SEQ:CH]), S["pend_ready"])
                            L.do(G.tensor_copy(pend[:, d, 2:6], Pc[:, LAT + e:TP:CH]), S["pend_ready"])
                            tt(ar[:, d, 1, :], rc, Pc, sig="rr_ready")
                        pool.wait_ge(S["til_ready"].h, 2 * (p + 1))
                        eye = ident.unsqueeze(1).to_broadcast([P, 12, P])
                        L.settle()
                        L.do(G.tensor_copy(xv, eye), S["x_init"])
                        L.do(G.tensor_copy(tvv, eye), S["x_init"])
                        for d in range(2):
                            pool.wait_ge(S["xi_ready"].h, 2 * p + d + 1)
                            pool.wait_ge(S["rope_ready"].h, 2 * (p + 1))
                            tt(qx[:, d, :], tq[:, LAT:TP], xi[:, d, :], sig="qx_ready")
                    for j in range(BLOCKS - MERGE0):
                        pool.wait_ge(S["w_hi"].h, j + 1)
                        raw = ring[:, (MERGE0 + j) % RING * 1024:((MERGE0 + j) % RING + 1) * 1024]
                        tt(wlo[j % 3], raw, whi[j % 3].bitcast(F32), ALU.subtract, sig="w_lo")

            for s in handles:
                nc.gpsimd.sem_clear(s)
            nc.all_engine_barrier()

        with nc.Block() as block:
            @block.sync
            def _(sp):
                sp.dma_start(x_out, xres[:, :]).then_inc(setup, 16)
                sp.wait_ge(setup, 48 + 5 + 16)


def constants():
    import numpy as np
    c = np.zeros((P, NCN), np.float32)

    def put(name, a):
        a = np.asarray(a, np.float32).reshape(P, -1)
        c[:, CN[name]:CN[name] + a.shape[1]] = a

    i = np.arange(P)
    put("ident", np.eye(P))
    put("ones", np.ones((P, P)))
    put("blk", i[:, None] // 64 == i[None, :] // 64)
    first = i % 32 < 16
    partner = np.where(first, i + 16, i - 16)
    perm = np.zeros((P, P))
    perm[partner, i] = np.where(first, -1.0, 1.0)
    put("perm", perm)
    t = np.arange(DEC)
    inv = np.float32(10000.0) ** (-np.arange(16, dtype=np.float32) / np.float32(16))
    pos = np.where((i % 64 < 32)[:, None], t[None, :] // 64, t[None, :] % 64).astype(np.float32)
    ang = pos * inv[i % 16][:, None]
    put("cos", np.cos(ang))
    put("sin", np.sin(ang))
    reset = np.ones((2, TP))
    for s0, n in ((0, SEQ), (LAT, DEC)):
        reset[0, s0:s0 + n:CH] = 0.0
        reset[1, s0 + CH - 1:s0 + n:CH] = 0.0
    reset[:, GAP] = 0.0
    put("reset", np.broadcast_to(reset, (P, 2, TP)))
    same = i[:, None] // CH == i[None, :] // CH
    s_, t_ = i[:, None], i[None, :]
    put("tri", np.stack([same & (s_ < t_), same & (s_ <= t_), same & (s_ > t_), same & (s_ >= t_)], 1))
    lev = []
    for lv in range(LEVELS):
        b = 1 << lv
        low = (s_ // (2 * b) == t_ // (2 * b)) & (s_ % (2 * b) >= b) & (t_ % (2 * b) < b)
        lev += [low, low.T]
    put("lev", np.stack(lev, 1))
    x = np.arange(-P, DEC)[None, :] - i[:, None]
    put("posd", np.maximum(x, 0))
    put("negd", np.maximum(-x, 0))
    put("diag", x == 0)
    put("xi", np.broadcast_to(np.stack([t + 1, DEC - t]), (P, 2, DEC)))
    w, w2 = (i % 64)[:, None], np.arange(64)[None, :]
    start = np.clip(w - 8, 0, 48)
    put("colmask", np.where((w2 >= start) & (w2 < start + 16), 0.0, -1e9))
    put("zp", np.stack([SEQ - 1 - i, i], 1))
    return c


def kernel(**inputs):
    import numpy as np
    import concourse.bacc as bacc
    from concourse.bass_utils import run_bass_kernel_spmd as run

    g = {k: np.asarray(v) for k, v in inputs.items()}
    cat, f32 = np.concatenate, np.float32

    def colblocks(w):
        n = w.shape[1] // P
        return w.reshape(8, P, n, P).transpose(2, 1, 0, 3).reshape(n, P, 1024)

    def units(u):
        return u.reshape(-1, 8, P, P).transpose(0, 2, 1, 3).reshape(-1, P, 1024)

    def tiles(w):
        return w.reshape(w.shape[0] // P, P, w.shape[1] // P, P).transpose(2, 0, 1, 3)

    def channels(a):
        return a.reshape(-1, P).T

    streams, params, packs = [], [], []
    for l in range(DEPTH):
        wi = colblocks(g["w_in"][l])
        wo = units(cat([tiles(g[n][l]) for n in ("w_o_rwkv", "w_o_na", "w_o_ret")], 1).reshape(-1, P, P))
        ada = g["ada_w"][l].reshape(4, 2, P, 12, 512).transpose(3, 0, 2, 1, 4).reshape(48, P, 1024)
        seq = [ada, wi[12:14]]
        for p in range(PAIRS):
            seq.append(wi[[p, 4 + p, 8 + p, 14 + p, 18 + p, 22 + p, 26 + p, 30 + p, 34 + p, 38 + p]])
        for m in range(0, 8, 2):
            a, b = [42 + 8 * i + m for i in range(3)], [43 + 8 * i + m for i in range(3)]
            j = 3 * (m // 2)
            seq += [wi[a[:2]], wo[j:j + 1], wi[[a[2], b[0]]], wo[j + 1:j + 2], wi[b[1:]], wo[j + 2:j + 3]]
        seq += [colblocks(g["w_out"][l])]
        up = colblocks(g["ffn_up"][l])
        seq += [up.reshape(2, FT, P, 1024).transpose(1, 0, 2, 3).reshape(2 * FT, P, 1024)]
        seq += [units(tiles(g["ffn_down"][l]).reshape(-1, P, P))]
        streams.append(cat(seq, 0))
        dec = g["ret_decay"][l]
        params.append(cat([
            channels(g["norm_mix_pre"][l]), channels(g["norm_mix_post"][l]), channels(g["norm_ffn_pre"][l]),
            channels(g["norm_ffn_post"][l]), channels(g["ada_b"][l]),
            g["rwkv_conv"][l].reshape(3, 14, P).transpose(2, 1, 0).reshape(P, 42),
            g["ffn_conv"][l].reshape(3, 44, P).transpose(2, 1, 0).reshape(P, 132),
            channels(g["rwkv_w0"][l]), channels(g["rwkv_a0"][l]), channels(g["rwkv_k_k"][l]),
            channels(g["rwkv_k_a"][l]), channels(g["rwkv_r_k"][l]), channels(g["rwkv_ln_g"][l]),
            channels(g["rwkv_ln_b"][l]), channels(g["ret_gn"][l]),
            channels(np.repeat(dec, 64, axis=1)), np.broadcast_to(dec.reshape(1, 16), (P, 16))], 1))
        rpb = g["na_rpb"][l][:, 4:11]
        rpb = np.pad(rpb, ((0, 0), (1, 1), (48, 49)))
        toep = np.stack([rpb[:, :, 63 - w:127 - w] for w in range(64)], 1)
        bias = cat([toep[:, :, 2:8], toep[:, :, 1:7]], 1)
        for p in range(PAIRS):
            hs, ch = slice(2 * p, 2 * p + 2), slice(p * P, (p + 1) * P)
            lora = cat([g["rwkv_w_up"][l][:, :, ch], g["rwkv_a_up"][l][:, :, ch]], 1).transpose(1, 0, 2)
            packs.append(cat([
                lora.reshape(P, 256), g["rwkv_g_up"][l][:, ch],
                g["cache_na_k"][0, l, hs].transpose(0, 2, 1).reshape(P, P),
                g["cache_na_v"][0, l, hs].transpose(1, 0, 2).reshape(P, P),
                bias[hs].transpose(1, 0, 2, 3).reshape(P, 768),
                g["state_rwkv"][0, l][:, hs].transpose(1, 3, 0, 2).reshape(P, 128),
                g["state_ret"][0, l][:, hs].transpose(1, 2, 0, 3).reshape(P, 128)], 1))

    xin = np.zeros((P, KT, TP), f32)
    xin[:, :, 0:SEQ] = g["x_prompt"][0].T.reshape(KT, P, SEQ).transpose(1, 0, 2)
    xin[:, :, LAT:] = g["x_sample"][0].T.reshape(KT, P, DEC).transpose(1, 0, 2)
    cc = np.stack([g["c_ctx"].reshape(KT, P).T, g["c"][0].reshape(KT, P).T], 2)
    ins = {
        "in_x": xin.reshape(P, -1), "in_w": np.stack(streams), "in_prm": np.stack(params),
        "in_pk": np.stack(packs).reshape(DEPTH, PAIRS, P, NPK), "in_cc": cc.reshape(P, -1), "in_const": constants(),
    }
    ins = {k: np.ascontiguousarray(v) for k, v in ins.items()}
    outs = {
        "out_x": (P, KT * TP), "out_nak": (DEPTH, PAIRS, P, SEQ), "out_nav": (DEPTH, PAIRS, SEQ, P),
        "out_srw": (DEPTH, PAIRS, P, 128), "out_srt": (DEPTH, PAIRS, P, 128),
    }
    nc = bacc.Bacc("TRN2", target_bir_lowering=False, num_devices=1)
    args = [nc.dram_tensor(k, v.shape, F32, kind="ExternalInput").ap() for k, v in ins.items()]
    args += [nc.dram_tensor(k, s, F32, kind="ExternalOutput").ap() for k, s in outs.items()]
    trunk(nc, *args)
    r = run(nc, [ins], core_ids=[0]).results[0]
    y = np.asarray(r["out_x"]).reshape(P, KT, TP).transpose(2, 1, 0).reshape(TP, D)
    k = np.asarray(r["out_nak"]).reshape(DEPTH, 8, 64, SEQ).transpose(0, 1, 3, 2)
    v = np.asarray(r["out_nav"]).reshape(DEPTH, PAIRS, SEQ, 2, 64).transpose(0, 1, 3, 2, 4).reshape(DEPTH, 8, SEQ, 64)
    rw = np.asarray(r["out_srw"]).reshape(DEPTH, PAIRS, 2, 64, 2, 64).transpose(0, 4, 1, 2, 5, 3)
    rt = np.asarray(r["out_srt"]).reshape(DEPTH, PAIRS, 2, 64, 2, 64).transpose(0, 4, 1, 2, 3, 5)
    full = np.ascontiguousarray
    return (full(y[0:SEQ][None]), full(y[LAT:][None]), full(k[None]), full(v[None]),
            full(rw.reshape(1, DEPTH, 2, 8, 64, 64)), full(rt.reshape(1, DEPTH, 2, 8, 64, 64)))
```
